# Optimizing a Trainium2 kernel written in Bass

```python
import jax, jax.numpy as jnp
from jax import lax
import numpy as np
import math

D_MODEL = 1024
BATCH = 1
SEQ = 512
DEPTH = 2

HEAD_DIM = 64
EPS = 1e-6
LRU_WIDTH = D_MODEL // 2
LRU_BLOCKS = 8
LRU_BLOCK = LRU_WIDTH // LRU_BLOCKS
LRU_CONV = 4
LRU_C = 8.0
SB_HEADS = 8
SB_WIDTH = SB_HEADS * HEAD_DIM
Q_BLOCK = 128
N_EVEN_SPLITS = 5
SWA_HEADS = D_MODEL // HEAD_DIM
SWA_KV_HEADS = 4
SWA_GROUP = SWA_HEADS // SWA_KV_HEADS
WINDOW = 128
D_FF = 2816
FFN_CONV = 3
N_EVEN = (DEPTH + 1) // 2
N_ODD = DEPTH // 2


def rms_norm(x, g):
    xf = x.astype(jnp.float32)
    y = xf * lax.rsqrt(jnp.mean(xf * xf, axis=-1, keepdims=True) + EPS)
    return (y * g.astype(jnp.float32)).astype(x.dtype)

def causal_dwconv(x, w, b):
    k_width, ch = w.shape
    y = lax.conv_general_dilated(
        x, w[:, None, :].astype(x.dtype), window_strides=(1,),
        padding=[(k_width - 1, 0)], dimension_numbers=("NWC", "WIO", "NWC"),
        feature_group_count=ch)
    return y + b.astype(x.dtype)

def adaln_params(c, w, b):
    m = jax.nn.silu(c) @ w + b
    return [t[:, None, :] for t in jnp.split(m, 6, axis=-1)]

def rg_lru(x, wa, ba, wx, bx, lam):
    bsz, seq, width = x.shape
    xb = x.reshape(bsz, seq, LRU_BLOCKS, LRU_BLOCK)
    r = jax.nn.sigmoid((jnp.einsum("bsnk,nkj->bsnj", xb, wa).reshape(bsz, seq, width) + ba).astype(jnp.float32))
    i = jax.nn.sigmoid((jnp.einsum("bsnk,nkj->bsnj", xb, wx).reshape(bsz, seq, width) + bx).astype(jnp.float32))
    log_a = -LRU_C * r * jax.nn.softplus(-lam.astype(jnp.float32))
    a = jnp.exp(log_a)
    u = jnp.sqrt(-jnp.expm1(2.0 * log_a)) * (i * x.astype(jnp.float32))

    def combine(e1, e2):
        a1, b1 = e1
        a2, b2 = e2
        return a1 * a2, a2 * b1 + b2

    _, h = lax.associative_scan(combine, (a, u), axis=1)
    return h.astype(x.dtype)

def stick_breaking(q, k, v):
    bsz, seq, heads, dh = q.shape
    nb = seq // Q_BLOCK
    scale = 1.0 / np.sqrt(dh)
    qb = q.reshape(bsz, nb, Q_BLOCK, heads, dh).transpose(1, 0, 3, 2, 4)
    kh = k.transpose(0, 2, 1, 3)
    vh = v.transpose(0, 2, 1, 3)
    kpos = jnp.arange(seq)

    def block(args):
        qi, blk = args
        z = jnp.einsum("bhqd,bhkd->bhqk", qi, kh).astype(jnp.float32) * scale
        qpos = blk * Q_BLOCK + jnp.arange(Q_BLOCK)
        mask = kpos[None, :] < qpos[:, None]
        sp = jnp.where(mask, jax.nn.softplus(z), 0.0)
        rev = lax.cumsum(sp, axis=3, reverse=True)
        w = jnp.exp(jnp.where(mask, z - rev, -jnp.inf))
        return jnp.einsum("bhqk,bhkd->bhqd", w.astype(v.dtype), vh)

    out = lax.map(block, (qb, jnp.arange(nb)))
    return out.transpose(1, 0, 3, 2, 4).reshape(bsz, seq, heads * dh)

def swa_sinks(q, k, v, sinks):
    bsz, seq, _, dh = q.shape
    nb = seq // WINDOW
    scale = 1.0 / np.sqrt(dh)
    qb = q.reshape(bsz, nb, WINDOW, SWA_KV_HEADS, SWA_GROUP, dh)

    def banded(t):
        tb = t.reshape(bsz, nb, WINDOW, SWA_KV_HEADS, dh)
        prev = jnp.concatenate([jnp.zeros_like(tb[:, :1]), tb[:, :-1]], axis=1)
        return jnp.concatenate([prev, tb], axis=2)

    kk, vv = banded(k), banded(v)
    s = jnp.einsum("bnqkgd,bnjkd->bnkgqj", qb, kk).astype(jnp.float32) * scale
    i = jnp.arange(WINDOW)[:, None]
    j = jnp.arange(2 * WINDOW)[None, :]
    band = (j > i) & (j <= i + WINDOW)
    blk = jnp.arange(nb)[:, None, None]
    mask = band[None] & ((j >= WINDOW)[None] | (blk > 0))
    s = jnp.where(mask[None, :, None, None], s, -jnp.inf)
    sink = sinks.astype(jnp.float32).reshape(SWA_KV_HEADS, SWA_GROUP)[None, None, :, :, None, None]
    m = jnp.maximum(jnp.max(s, axis=-1, keepdims=True), sink)
    p = jnp.exp(s - m)
    p = p / (jnp.sum(p, axis=-1, keepdims=True) + jnp.exp(sink - m))
    out = jnp.einsum("bnkgqj,bnjkd->bnqkgd", p.astype(v.dtype), vv)
    return out.reshape(bsz, seq, SWA_HEADS * dh)

def conv_ffn(h, w_gate, w_up, conv_w, conv_b, w_down):
    a = causal_dwconv(h @ w_gate, conv_w, conv_b)
    return (jax.nn.silu(a) * (h @ w_up)) @ w_down

def first_inputs(seed: int = 0) -> dict:
    key = jax.random.key(seed)
    ks = iter(jax.random.split(key, 40))

    def nrm(shape, scale):
        return jax.random.normal(next(ks), shape, jnp.float32) * scale

    d = D_MODEL
    u = jax.random.uniform(next(ks), (N_EVEN, LRU_WIDTH), jnp.float32, minval=0.9, maxval=0.999)
    a0 = u ** (1.0 / LRU_C)
    lam = jnp.log(a0) - jnp.log1p(-a0)
    return {
        "x": nrm((BATCH, SEQ, d), 1.0),
        "c": nrm((BATCH, d), 1.0),
        "ada_w": nrm((DEPTH, d, 6 * d), 0.5 * d ** -0.5),
        "ada_b": nrm((DEPTH, 6 * d), 0.02),
        "norm_mix_g": 1.0 + nrm((DEPTH, d), 0.02),
        "norm_ffn_g": 1.0 + nrm((DEPTH, d), 0.02),
        "ev_w_in": nrm((N_EVEN, d, N_EVEN_SPLITS * LRU_WIDTH), d ** -0.5),
        "ev_conv_w": nrm((N_EVEN, LRU_CONV, LRU_WIDTH), LRU_CONV ** -0.5),
        "ev_conv_b": nrm((N_EVEN, LRU_WIDTH), 0.02),
        "ev_wa": nrm((N_EVEN, LRU_BLOCKS, LRU_BLOCK, LRU_BLOCK), LRU_BLOCK ** -0.5),
        "ev_ba": nrm((N_EVEN, LRU_WIDTH), 0.02),
        "ev_wx": nrm((N_EVEN, LRU_BLOCKS, LRU_BLOCK, LRU_BLOCK), LRU_BLOCK ** -0.5),
        "ev_bx": nrm((N_EVEN, LRU_WIDTH), 0.02),
        "ev_lam": lam,
        "ev_qn_g": 1.0 + nrm((N_EVEN, HEAD_DIM), 0.02),
        "ev_kn_g": 1.0 + nrm((N_EVEN, HEAD_DIM), 0.02),
        "ev_w_out": nrm((N_EVEN, LRU_WIDTH + SB_WIDTH, d), (LRU_WIDTH + SB_WIDTH) ** -0.5),
        "od_w_in": nrm((N_ODD, d, (SWA_HEADS + 2 * SWA_KV_HEADS) * HEAD_DIM), d ** -0.5),
        "od_qn_g": 1.0 + nrm((N_ODD, HEAD_DIM), 0.02),
        "od_kn_g": 1.0 + nrm((N_ODD, HEAD_DIM), 0.02),
        "od_sinks": nrm((N_ODD, SWA_HEADS), 1.0),
        "od_w_out": nrm((N_ODD, SWA_HEADS * HEAD_DIM, d), (SWA_HEADS * HEAD_DIM) ** -0.5),
        "ffn_w_gate": nrm((DEPTH, d, D_FF), d ** -0.5),
        "ffn_w_up": nrm((DEPTH, d, D_FF), d ** -0.5),
        "ffn_conv_w": nrm((DEPTH, FFN_CONV, D_FF), FFN_CONV ** -0.5),
        "ffn_conv_b": nrm((DEPTH, D_FF), 0.02),
        "ffn_w_down": nrm((DEPTH, D_FF, d), D_FF ** -0.5),
    }

def first_block(x, c, ada_w, ada_b, norm_mix_g, norm_ffn_g,
              ev_w_in, ev_conv_w, ev_conv_b, ev_wa, ev_ba, ev_wx, ev_bx, ev_lam,
              ev_qn_g, ev_kn_g, ev_w_out,
              od_w_in, od_qn_g, od_kn_g, od_sinks, od_w_out,
              ffn_w_gate, ffn_w_up, ffn_conv_w, ffn_conv_b, ffn_w_down):
    bsz, seq, _ = x.shape
    for layer in range(DEPTH):
        sh1, sc1, g1, sh2, sc2, g2 = adaln_params(c, ada_w[layer], ada_b[layer])
        h = rms_norm(x, norm_mix_g[layer]) * (1.0 + sc1) + sh1
        if layer % 2 == 0:
            e = layer // 2
            xr, gr, q, k, v = jnp.split(h @ ev_w_in[e], N_EVEN_SPLITS, axis=-1)
            xr = causal_dwconv(xr, ev_conv_w[e], ev_conv_b[e])
            hr = rg_lru(xr, ev_wa[e], ev_ba[e], ev_wx[e], ev_bx[e], ev_lam[e])
            ya = hr * jax.nn.gelu(gr)
            q = rms_norm(q.reshape(bsz, seq, SB_HEADS, HEAD_DIM), ev_qn_g[e])
            k = rms_norm(k.reshape(bsz, seq, SB_HEADS, HEAD_DIM), ev_kn_g[e])
            v = v.reshape(bsz, seq, SB_HEADS, HEAD_DIM)
            yb = stick_breaking(q, k, v)
            mix = jnp.concatenate([ya, yb], axis=-1) @ ev_w_out[e]
        else:
            o = layer // 2
            p = h @ od_w_in[o]
            q_w = SWA_HEADS * HEAD_DIM
            kv_w = SWA_KV_HEADS * HEAD_DIM
            q = rms_norm(p[..., :q_w].reshape(bsz, seq, SWA_HEADS, HEAD_DIM), od_qn_g[o])
            k = rms_norm(p[..., q_w:q_w + kv_w].reshape(bsz, seq, SWA_KV_HEADS, HEAD_DIM), od_kn_g[o])
            v = p[..., q_w + kv_w:].reshape(bsz, seq, SWA_KV_HEADS, HEAD_DIM)
            mix = swa_sinks(q, k, v, od_sinks[o]) @ od_w_out[o]
        x = x + g1 * mix
        h = rms_norm(x, norm_ffn_g[layer]) * (1.0 + sc2) + sh2
        x = x + g2 * conv_ffn(h, ffn_w_gate[layer], ffn_w_up[layer], ffn_conv_w[layer],
                              ffn_conv_b[layer], ffn_w_down[layer])
    return x


N_MIXERS = 2
N_A = (DEPTH + 1) // 2
N_B = DEPTH // 2
N_SUB = 3
FFN_RES = 0.5

MLA_HEADS = 16
Q_LORA = 384
KV_LORA = 256
QK_NOPE = 64
QK_ROPE = 32
V_HEAD = 64
ROPE_THETA = 10000.0

DIL_GROUPS = ((128, 1), (512, 4), (2048, 16))
N_GROUPS = 3
DIL_HEADS = 16
DIL_HEAD_DIM = 64
DIL_BLOCK = 128
DIL_WIDTH = DIL_HEADS * DIL_HEAD_DIM

N_BUCKETS = 32
MAX_DISTANCE = 2048


def rmsnorm(x, g):
    xf = x.astype(jnp.float32)
    y = xf * lax.rsqrt(jnp.mean(xf * xf, axis=-1, keepdims=True) + EPS)
    return (y * g.astype(jnp.float32)).astype(x.dtype)

def swiglu(h, w_gate, w_up, w_down):
    return (jax.nn.silu(h @ w_gate) * (h @ w_up)) @ w_down

def rope(x, pos):
    half = x.shape[-1] // 2
    freqs = ROPE_THETA ** (-jnp.arange(half, dtype=jnp.float32) / half)
    ang = pos[:, None] * freqs[None, :]
    cos = jnp.cos(ang)[None, :, None, :]
    sin = jnp.sin(ang)[None, :, None, :]
    x1 = x[..., :half].astype(jnp.float32)
    x2 = x[..., half:].astype(jnp.float32)
    return jnp.concatenate([x1 * cos - x2 * sin, x1 * sin + x2 * cos], axis=-1).astype(x.dtype)

def causal_block_attention(q, k, v, scale):
    B, S, H, dq = q.shape
    nb = S // Q_BLOCK
    qb = q.reshape(B, nb, Q_BLOCK, H, dq).transpose(1, 0, 3, 2, 4)
    kt = k.transpose(0, 2, 1, 3)
    vt = v.transpose(0, 2, 1, 3)
    kpos = jnp.arange(S)

    def one_block(args):
        qi, n = args
        s = jnp.einsum('bhqd,bhkd->bhqk', qi, kt).astype(jnp.float32) * scale
        qpos = n * Q_BLOCK + jnp.arange(Q_BLOCK)
        s = jnp.where(kpos[None, :] <= qpos[:, None], s, -jnp.inf)
        p = jax.nn.softmax(s, axis=-1).astype(vt.dtype)
        return jnp.einsum('bhqk,bhkd->bhqd', p, vt)

    out = lax.map(one_block, (qb, jnp.arange(nb)))
    return out.transpose(1, 0, 3, 2, 4).reshape(B, S, H, v.shape[-1])

def mla(h, w_in, q_norm, w_q_up, kv_norm, w_kv_up, w_o):
    B, S, _ = h.shape
    lat = h @ w_in
    cq = lat[..., :Q_LORA]
    ckv = lat[..., Q_LORA:Q_LORA + KV_LORA]
    k_rope = lat[..., Q_LORA + KV_LORA:][:, :, None, :]
    q = (rmsnorm(cq, q_norm) @ w_q_up).reshape(B, S, MLA_HEADS, QK_NOPE + QK_ROPE)
    kv = (rmsnorm(ckv, kv_norm) @ w_kv_up).reshape(B, S, MLA_HEADS, QK_NOPE + V_HEAD)
    pos = jnp.arange(S, dtype=jnp.float32)
    q = jnp.concatenate([q[..., :QK_NOPE], rope(q[..., QK_NOPE:], pos)], axis=-1)
    k_rope = jnp.broadcast_to(rope(k_rope, pos), (B, S, MLA_HEADS, QK_ROPE))
    k = jnp.concatenate([kv[..., :QK_NOPE], k_rope.astype(kv.dtype)], axis=-1)
    v = kv[..., QK_NOPE:]
    o = causal_block_attention(q, k, v, (QK_NOPE + QK_ROPE) ** -0.5)
    return o.reshape(B, S, MLA_HEADS * V_HEAD) @ w_o

def t5_bucket(dist):
    max_exact = N_BUCKETS // 2
    d = jnp.maximum(dist, 1).astype(jnp.float32)
    large = max_exact + (jnp.log(d / max_exact) / math.log(MAX_DISTANCE / max_exact)
                         * (N_BUCKETS - max_exact)).astype(jnp.int32)
    large = jnp.minimum(large, N_BUCKETS - 1)
    return jnp.where(dist < max_exact, dist, large)

def strided_window_attention(q, k, v, dilation, span, bias_table):
    B, S, H, E = q.shape
    L = S // dilation
    nb = -(-L // DIL_BLOCK)
    Lp = nb * DIL_BLOCK
    qs = q.reshape(B, L, dilation, H, E)
    qb = jnp.pad(qs, ((0, 0), (0, Lp - L), (0, 0), (0, 0), (0, 0))).reshape(B, nb, DIL_BLOCK, dilation, H, E)

    def windows(t):
        tp = jnp.pad(t.reshape(B, L, dilation, H, E),
                     ((0, 0), (DIL_BLOCK, Lp - L), (0, 0), (0, 0), (0, 0)))
        tp = tp.reshape(B, nb + 1, DIL_BLOCK, dilation, H, E)
        return jnp.concatenate([tp[:, :-1], tp[:, 1:]], axis=2)

    kw, vw = windows(k), windows(v)
    s = jnp.einsum('bnqrhe,bnkrhe->bnrhqk', qb, kw).astype(jnp.float32) * (E ** -0.5)
    iq = jnp.arange(DIL_BLOCK)[:, None]
    ik = jnp.arange(2 * DIL_BLOCK)[None, :]
    rel = DIL_BLOCK + iq - ik
    in_window = (rel >= 0) & (rel <= span)
    bucket = t5_bucket(jnp.maximum(rel, 0) * dilation)
    bias = jnp.transpose(bias_table[bucket], (2, 0, 1)).astype(jnp.float32)
    key_m = (jnp.arange(nb)[:, None] - 1) * DIL_BLOCK + jnp.arange(2 * DIL_BLOCK)[None, :]
    valid = in_window[None] & (key_m >= 0)[:, None, :]
    logits = jnp.where(valid[None, :, None, None], s + bias, -jnp.inf)
    lse = jax.nn.logsumexp(logits, axis=-1)
    p = jnp.exp(logits - lse[..., None]).astype(v.dtype)
    o = jnp.einsum('bnrhqk,bnkrhe->bnqrhe', p, vw)
    o = o.reshape(B, Lp, dilation, H, E)[:, :L].reshape(B, S, H, E)
    lse = jnp.transpose(lse, (0, 1, 4, 2, 3)).reshape(B, Lp, dilation, H)[:, :L].reshape(B, S, H)
    return o, lse

def dilated_attention(h, w_in, w_o, rel_bias):
    B, S, _ = h.shape
    proj = (h @ w_in).reshape(B, S, N_GROUPS, 3, DIL_HEADS, DIL_HEAD_DIM)
    outs, lses = [], []
    for g, (window, dilation) in enumerate(DIL_GROUPS):
        o, lse = strided_window_attention(
            proj[:, :, g, 0], proj[:, :, g, 1], proj[:, :, g, 2],
            dilation, window // dilation, rel_bias[:, g * DIL_HEADS:(g + 1) * DIL_HEADS])
        outs.append(o)
        lses.append(lse)
    alpha = jax.nn.softmax(jnp.stack(lses, axis=0), axis=0)
    o = jnp.sum(alpha[..., None] * jnp.stack(outs, axis=0).astype(jnp.float32), axis=0)
    return o.astype(h.dtype).reshape(B, S, DIL_WIDTH) @ w_o

def sandwich(x, fn, pre_g, post_g, shift, scale, gate, res_w):
    hn = rmsnorm(x, pre_g) * (1 + scale[:, None, :]) + shift[:, None, :]
    y = rmsnorm(fn(hn), post_g)
    return x + res_w * gate[:, None, :] * y

def second_inputs(seed: int = 0) -> dict:
    key = jax.random.key(seed)
    ks = jax.random.split(key, 20)
    D = D_MODEL
    nrm = lambda k, shape, fan: jax.random.normal(k, shape, jnp.float32) * fan ** -0.5
    return {
        "x": jax.random.normal(ks[0], (BATCH, SEQ, D), jnp.float32),
        "c": jax.random.normal(ks[1], (BATCH, D), jnp.float32),
        "norm_pre": 1.0 + 0.05 * jax.random.normal(ks[2], (DEPTH, N_SUB, D), jnp.float32),
        "norm_post": 1.0 + 0.05 * jax.random.normal(ks[3], (DEPTH, N_SUB, D), jnp.float32),
        "w_mod": nrm(ks[4], (DEPTH, D, N_SUB * 3 * D), D) * 0.5,
        "b_mod": 0.02 * jax.random.normal(ks[5], (DEPTH, N_SUB * 3 * D), jnp.float32),
        "ffn_w_gate": nrm(ks[6], (DEPTH, 2, D, D_FF), D),
        "ffn_w_up": nrm(ks[7], (DEPTH, 2, D, D_FF), D),
        "ffn_w_down": nrm(ks[8], (DEPTH, 2, D_FF, D), D_FF),
        "mla_w_in": nrm(ks[9], (N_A, D, Q_LORA + KV_LORA + QK_ROPE), D),
        "mla_q_norm": 1.0 + 0.05 * jax.random.normal(ks[10], (N_A, Q_LORA), jnp.float32),
        "mla_w_q_up": nrm(ks[11], (N_A, Q_LORA, MLA_HEADS * (QK_NOPE + QK_ROPE)), Q_LORA),
        "mla_kv_norm": 1.0 + 0.05 * jax.random.normal(ks[12], (N_A, KV_LORA), jnp.float32),
        "mla_w_kv_up": nrm(ks[13], (N_A, KV_LORA, MLA_HEADS * (QK_NOPE + V_HEAD)), KV_LORA),
        "mla_w_o": nrm(ks[14], (N_A, MLA_HEADS * V_HEAD, D), MLA_HEADS * V_HEAD),
        "dil_w_in": nrm(ks[15], (N_B, D, N_GROUPS * 3 * DIL_WIDTH), D),
        "dil_w_o": nrm(ks[16], (N_B, DIL_WIDTH, D), DIL_WIDTH),
        "rel_bias": 0.5 * jax.random.normal(ks[17], (N_BUCKETS, N_GROUPS * DIL_HEADS), jnp.float32),
    }

def second_block(x, c, norm_pre, norm_post, w_mod, b_mod, ffn_w_gate, ffn_w_up, ffn_w_down,
              mla_w_in, mla_q_norm, mla_w_q_up, mla_kv_norm, mla_w_kv_up, mla_w_o,
              dil_w_in, dil_w_o, rel_bias):
    B = x.shape[0]
    for i in range(DEPTH):
        mod = (jax.nn.silu(c) @ w_mod[i] + b_mod[i]).reshape(B, N_SUB, 3, D_MODEL)

        def ffn_first(h, i=i):
            return swiglu(h, ffn_w_gate[i, 0], ffn_w_up[i, 0], ffn_w_down[i, 0])

        def ffn_second(h, i=i):
            return swiglu(h, ffn_w_gate[i, 1], ffn_w_up[i, 1], ffn_w_down[i, 1])

        if i % N_MIXERS == 0:
            a = i // N_MIXERS
            def mixer(h, a=a):
                return mla(h, mla_w_in[a], mla_q_norm[a], mla_w_q_up[a],
                           mla_kv_norm[a], mla_w_kv_up[a], mla_w_o[a])
        else:
            b = i // N_MIXERS
            def mixer(h, b=b):
                return dilated_attention(h, dil_w_in[b], dil_w_o[b], rel_bias)

        x = sandwich(x, ffn_first, norm_pre[i, 0], norm_post[i, 0],
                     mod[:, 0, 0], mod[:, 0, 1], mod[:, 0, 2], FFN_RES)
        x = sandwich(x, mixer, norm_pre[i, 1], norm_post[i, 1],
                     mod[:, 1, 0], mod[:, 1, 1], mod[:, 1, 2], 1.0)
        x = sandwich(x, ffn_second, norm_pre[i, 2], norm_post[i, 2],
                     mod[:, 2, 0], mod[:, 2, 1], mod[:, 2, 2], FFN_RES)
    return x


def setup_inputs(seed=0):
    out = dict(first_inputs(seed))
    for name, value in second_inputs(seed + 1).items():
        if name != "x":
            out[name + "_2"] = value
    return out


def reference(
    x, c, ada_w, ada_b, norm_mix_g, norm_ffn_g, ev_w_in, ev_conv_w, ev_conv_b, ev_wa, ev_ba,
    ev_wx, ev_bx, ev_lam, ev_qn_g, ev_kn_g, ev_w_out, od_w_in, od_qn_g, od_kn_g, od_sinks,
    od_w_out, ffn_w_gate, ffn_w_up, ffn_conv_w, ffn_conv_b, ffn_w_down, c_2, norm_pre_2,
    norm_post_2, w_mod_2, b_mod_2, ffn_w_gate_2, ffn_w_up_2, ffn_w_down_2, mla_w_in_2,
    mla_q_norm_2, mla_w_q_up_2, mla_kv_norm_2, mla_w_kv_up_2, mla_w_o_2, dil_w_in_2, dil_w_o_2,
    rel_bias_2,
):
    x = first_block(
        x, c, ada_w, ada_b, norm_mix_g, norm_ffn_g, ev_w_in, ev_conv_w, ev_conv_b, ev_wa, ev_ba,
        ev_wx, ev_bx, ev_lam, ev_qn_g, ev_kn_g, ev_w_out, od_w_in, od_qn_g, od_kn_g, od_sinks,
        od_w_out, ffn_w_gate, ffn_w_up, ffn_conv_w, ffn_conv_b, ffn_w_down,
    )
    return second_block(
        x, c_2, norm_pre_2, norm_post_2, w_mod_2, b_mod_2, ffn_w_gate_2, ffn_w_up_2,
        ffn_w_down_2, mla_w_in_2, mla_q_norm_2, mla_w_q_up_2, mla_kv_norm_2, mla_w_kv_up_2,
        mla_w_o_2, dil_w_in_2, dil_w_o_2, rel_bias_2,
    )


_drawn_inputs = setup_inputs


def setup_inputs(seed=0):
    import zlib

    import numpy as np

    out = dict(_drawn_inputs(seed))
    spreads = {}
    factors = {'norm_mix_g': 8.0,
     'norm_ffn_g': 6.512,
     'ev_conv_b': 3.673,
     'ev_ba': 8.0,
     'ev_bx': 8.0,
     'ev_qn_g': 8.0,
     'ev_kn_g': 8.0,
     'od_qn_g': 8.0,
     'od_kn_g': 8.0,
     'od_sinks': 60.288,
     'ffn_conv_b': 8.0,
     'mla_q_norm_2': 64.0,
     'mla_kv_norm_2': 26.176,
     'norm_pre_2': 8.0,
     'norm_post_2': 8.0,
     'b_mod_2': 8.0,
     'ffn_w_gate_2': 3.416,
     'ffn_w_up_2': 3.176,
     'ffn_w_down_2': 3.186,
     'mla_w_in_2': 3.182,
     'mla_w_q_up_2': 3.504,
     'mla_w_kv_up_2': 3.199,
     'mla_w_o_2': 3.22,
     'dil_w_in_2': 3.238,
     'dil_w_o_2': 3.248,
     'rel_bias_2': 36.19}
    for name, (base, spread) in spreads.items():
        noise = np.random.default_rng([zlib.crc32(name.encode()), seed]).standard_normal(out[name].shape)
        drawn = base * np.exp(spread * noise) if base else spread * noise
        out[name] = __import__('jax').numpy.asarray(drawn.astype(out[name].dtype))
    for name, factor in factors.items():
        out[name] = (out[name] * factor).astype(out[name].dtype)
    return out
```

```python
import math
from contextlib import ExitStack

import numpy as np

import concourse.bass as bass
from concourse import mybir

F32 = mybir.dt.float32
F32R = mybir.dt.float32r
ACT = mybir.ActivationFunctionType
ALU = mybir.AluOpType
AX = mybir.AxisListType

EPS = 1e-6
NEG = -float(2.0 ** 100)
S = 512
P = 128
BT = 8
RAW, SPLIT = 5, 3
MLA_SCALE = 96.0 ** -0.5


def even_groups():
    gs = [(8, [("ev_in", 0), ("ev_in", 4), ("ev_in", 1), ("ev_in", 5)]),
          (8, [("ev_in", 2), ("ev_in", 6), ("ev_in", 3), ("ev_in", 7)]),
          (8, [("ev_in", 16 + i) for i in range(4)])]
    gs += [(8, [("ev_in", 8 + i)]) for i in range(8)]
    return gs + [(8, [("ev_out", i)]) for i in range(8)]


def odd_groups():
    gs = [(8, [("od_in", i) for i in range(4)])]
    gs += [(8, [("od_in", i)]) for i in range(4, 10)]
    gs += [(8, [("od_in", 10), ("od_in", 11)])]
    return gs + [(8, [("od_out", i)]) for i in range(8)]


def ffn_groups(tag):
    gs = []
    for half in (0, 1):
        at = 11 * half
        if half == 0:
            gs.append((8, [(tag + "g", 0), (tag + "u", 0), (tag + "g", 1), (tag + "u", 1)]))
            at = 2
        for i in range(at, 11 * half + 11):
            gs.append((8, [(tag + "g", i), (tag + "u", i)]))
        gs += [(11, [(tag + "d%d" % half, i)]) for i in range(8)]
    return gs


def mla_groups():
    gs = [(8, [("mla_in", i) for i in range(6)])]
    gs += [(2, [("mla_v", 4 * f + i) for i in range(4)]) for f in range(2)]
    for h in range(16):
        gs.append((3, [("mla_q", h)]))
        if h % 2 == 0:
            gs.append((2, [("mla_k", h // 2)]))
    return gs + [(8, [("mla_o", i)]) for i in range(8)]


def dil_groups():
    gs = []
    for c in range(8):
        tiles = [("dil_in", 72 * 0 + 24 * g + 8 * t + c) for g in range(3) for t in range(3)]
        if c == 0:
            gs.append((8, tiles[:4]))
            tiles = tiles[4:]
        gs += [(8, [t]) for t in tiles]
    return gs + [(8, [("dil_o", i)]) for i in range(8)]


def plan():
    gs = even_groups() + ffn_groups("f0") + odd_groups() + ffn_groups("f1")
    gs += ffn_groups("a0") + mla_groups() + ffn_groups("a1")
    gs += ffn_groups("b0") + dil_groups() + ffn_groups("b1")
    return gs


def tile_list():
    return [(name, k, m) for nk, cols in plan() for k in range(nk) for name, m in cols]


def columns():
    at, out = 0, {}
    for name, width in [
        ("c", 8), ("c2", 8), ("ada_b", 96), ("mix_g", 16), ("ffn_g", 16), ("cw", 16), ("cb", 4),
        ("ba", 4), ("bx", 4), ("lam", 4), ("evq", 1), ("evk", 1), ("odq", 1), ("odk", 1),
        ("fcw", 132), ("fcb", 44), ("pre", 48), ("post", 48), ("b_mod", 144), ("mq", 3), ("mkv", 2),
        ("sinks", 16),
    ]:
        out[name] = (at, width)
        at += width
    return out, at


def const_arrays():
    i = np.arange(P)
    c = {}
    c["ident"] = np.eye(P)
    c["ones"] = np.ones((P, P))
    c["blk"] = (i[:, None] // 64 == i[None, :] // 64) * 1.0
    c["later"] = (i[:, None] > i[None, :]) * 1.0
    c["tri"] = (i[:, None] < i[None, :]) * 1.0
    c["caus"] = np.where(i[None, :] <= i[:, None], 0.0, NEG)
    j = np.arange(256)
    c["band"] = np.where((j[None, :] > i[:, None]) & (j[None, :] <= i[:, None] + 128), 0.0, NEG)
    c["adiag"] = (i[:, None] // 32 == np.arange(4)[None, :]) * 1.0
    sel = np.zeros((P, P))
    sel[0, :64] = 1.0
    sel[1, 64:] = 1.0
    c["sel"] = sel
    half = 16
    freqs = np.float32(10000.0) ** (-np.arange(half, dtype=np.float32) / np.float32(half))
    ang = (np.arange(S, dtype=np.float32)[:, None] * freqs[None, :].astype(np.float32)).astype(np.float64)
    cos, sin = np.cos(ang).T, np.sin(ang).T
    trig = np.zeros((P, S))
    trig[64:80], trig[80:96] = cos, cos
    trig[96:112], trig[112:128] = -sin, sin
    c["trig"] = trig
    return {k: v.astype(np.float32) for k, v in c.items()}


CONST_WIDTHS = [("ident", 128), ("ones", 128), ("blk", 128), ("later", 128), ("tri", 128), ("caus", 128),
                ("band", 256), ("adiag", 4), ("sel", 128)]


def bucket(dist):
    d = np.maximum(dist, 1).astype(np.float32)
    large = 16 + (np.log(d / np.float32(16)) / np.float32(math.log(2048 / 16)) * np.float32(16)).astype(np.int32)
    return np.where(dist < 16, dist, np.minimum(large, 31))


def onehots():
    def table(rel, dil):
        ok = (rel >= 0) & (rel <= 128)
        b = np.where(ok, bucket(np.maximum(rel, 0) * dil), 32)
        return (np.arange(33)[:, None] == b[None, :]).astype(np.float32)

    o0 = table(np.arange(384) - 127, 1)
    o1 = table(np.arange(256) - 127, 4)
    o2 = table(np.arange(64) - 31, 16)
    return np.concatenate([o0, o1, o2], axis=1)


class Queue:

    def __init__(self, sem):
        self.sem, self.n, self.ops, self.seen = sem, 0, [], {}

    def do(self, fn, *waits, inc=True):
        need = []
        for w in flat(waits):
            key, sem, value = w
            if self.seen.get(key, 0) < value:
                self.seen[key] = value
                need.append((sem, value))
        self.ops.append((need, fn, 1 if inc else 0))
        if inc:
            self.n += 1
            return (id(self), self.sem, self.n)
        return None

    def dma(self, out, in_, sem, count, *waits):
        need = []
        for w in flat(waits):
            key, s, value = w
            if self.seen.get(key, 0) < value:
                self.seen[key] = value
                need.append((s, value))
        self.ops.append((need, lambda e: e.dma_start(out, in_).then_inc(sem, 16), 0))
        return (id(sem), sem, 16 * count)

    def play(self, eng):
        for need, fn, inc in self.ops:
            for sem, value in need:
                eng.wait_ge(sem, value)
            ins = fn(eng)
            if inc:
                ins.then_inc(self.sem, 1)


def flat(x):
    if x is None:
        return []
    if isinstance(x, tuple) and len(x) == 3 and isinstance(x[2], int):
        return [x]
    return [y for z in x for y in flat(z)]


class Ring:

    def __init__(self, bufs):
        self.bufs, self.rel, self.at = bufs, [[] for _ in bufs], 0

    def get(self):
        i = self.at
        self.at = (i + 1) % len(self.bufs)
        return i, self.bufs[i], self.rel[i]

    def put(self, i, *tokens):
        self.rel[i] = list(tokens)

    def all(self):
        return list(self.rel)


def interleave(*gens):
    live = list(gens)
    while live:
        for g in list(live):
            try:
                next(g)
            except StopIteration:
                live.remove(g)


def weave(main, side, every=1):
    n, live = 0, True
    for _ in main:
        n += 1
        if live and n % every == 0:
            live = next(side, "end") != "end"
    for _ in side:
        pass


def program(nc, xt, wst, mst, vec, cst, trig, oh, tab, wax, out, scratch):
    with ExitStack() as ctx:
        sem = lambda n: ctx.enter_context(nc.semaphore(n))
        base = 16512
        limit = 229368
        pos = [base]
        ctx.enter_context(nc.sbuf_tensor("arena", [P, (limit - base) // 4 - 16], F32))

        def at(name, offset, shape, dt=F32):
            n = 4
            for s in shape[1:]:
                n *= s
            assert offset + n <= limit, (name, offset + n, limit)
            return nc.alloc_sbuf_tensor_at(name, shape, dt, offset=offset)

        def sb(name, shape, dt=F32):
            n = 4
            for s in shape[1:]:
                n *= s
            t = at(name, pos[0], shape, dt)
            pos[0] += (n + 31) // 32 * 32
            return t

        cols, ncols = columns()
        pe, dve, act, pool, sp = (Queue(sem("s_" + n)) for n in ("pe", "dve", "act", "pool", "sp"))

        X = sb("X", [P, 8, S])
        HH = sb("HH", [P, 8, S], F32R)
        HL = sb("HL", [P, 8, S], F32R)
        wraw = sb("wraw", [P, RAW, BT * 128])
        whi = sb("whi", [P, SPLIT, BT * 128], F32R)
        wlo = sb("wlo", [P, SPLIT, BT * 128], F32R)
        mraw = sb("mraw", [P, 2, 1024])
        macc_off = pos[0]
        macc = sb("macc", [P, 1024])
        V = sb("V", [P, ncols])
        C = {}
        for n, w in CONST_WIDTHS:
            C[n] = sb("c_" + n, [P, w])
        identr = sb("identr", [P, P], F32R)
        causr = sb("causr", [P, P], F32R)
        bandr = sb("bandr", [P, 256], F32R)
        SILU = sb("SILU", [P, 16])
        MOD = sb("MOD", [P, 30, 8])
        AM = sb("AM", [P, 10, 8])
        GM = sb("GM", [P, 6, 8])
        CF = sb("CF", [P, 4])
        QS = sb("QS", [P, 2])
        EPSC = sb("EPSC", [P, 1])
        SQ = sb("SQ", [P, S])
        RS = sb("RS", [P, 2, S])
        TT = sb("TT", [P, 4, S])
        small = sb("small", [P, 160])
        ph = pos[0]
        ps = ctx.enter_context(nc.psum_tensor("ps", [P, 8, 512], F32))
        print("phase bytes", limit - ph) if False else None

        T = Ring([TT[:, i, :] for i in range(4)])
        RSR = Ring([RS[:, i, :] for i in range(2)])
        PB = [None]

        def banks(*idx):
            r = Ring([ps[:, i, :] for i in idx])
            r.idx = idx
            r.rel = [bankrel[i] for i in idx]
            for j, i in enumerate(idx):
                r.rel[j] = list(bankrel[i])
            return r

        bankrel = [[] for _ in range(8)]

        def bput(r, i, *tokens):
            r.put(i, *tokens)
            bankrel[r.idx[i]] = list(tokens)

        def col(name, i=0, w=1):
            a = cols[name][0] + i
            return V[:, a:a + w]

        def mm(o, l, r, start, stop, *waits, inc=False, skip=False):
            return pe.do(lambda e: e.matmul(o, l, r, start=start, stop=stop, skip_group_check=skip), *waits, inc=inc)

        def tpose(o, i, ident, *waits, inc=False):
            return pe.do(lambda e: e.transpose(o, i, ident), *waits, inc=inc)

        def fn(o, i, f, *waits, scale=1.0, bias=0.0, acc=None):
            if acc is None:
                return act.do(lambda e: e.activation(o, i, f, bias=bias, scale=scale), *waits)
            return act.do(lambda e: e.activation(o, i, f, bias=bias, scale=scale, accum_out=acc), *waits)

        def tt(q, o, a, b, op, *waits):
            return q.do(lambda e: e.tensor_tensor(o, a, b, op), *waits)

        def ts(q, o, a, s1, s2, op0, op1, *waits):
            if s2 is None:
                return q.do(lambda e: e.tensor_scalar(o, a, s1, None, op0), *waits)
            return q.do(lambda e: e.tensor_scalar(o, a, s1, s2, op0, op1), *waits)

        def stt(o, a, s, b, op0, op1, *waits):
            return dve.do(lambda e: e.scalar_tensor_tensor(o, a, s, b, op0, op1), *waits)

        def recip(o, i, *waits):
            return dve.do(lambda e: e.reciprocal(o, i), *waits)

        def cp(q, o, i, *waits):
            return q.do(lambda e: e.tensor_copy(o, i), *waits)

        s_c = [sem("s_c%d" % i) for i in range(8)]
        s_c1 = s_c[0]
        t_vec = sp.dma(V[:], vec, s_c[0], 1)
        t_x = sp.dma(X[:], xt, s_c[1], 1)
        t_cst = []
        a = 0
        s_cc = [sem("s_cc%d" % i) for i in range(len(CONST_WIDTHS))]
        for q, (n, w) in enumerate(CONST_WIDTHS):
            t_cst.append(sp.dma(C[n][:], cst[:, a:a + w], s_cc[q], 1))
            a += w
        t_const = {n: t_cst[q] for q, (n, w) in enumerate(CONST_WIDTHS)}

        tiles = tile_list()
        nblocks = (len(tiles) + BT - 1) // BT
        s_w = [sem("s_w%d" % i) for i in range(RAW)]
        W = {"tile": 0, "dma": 0, "split": 0}
        w_load, w_hi, w_lo, w_pe = {}, {}, {}, {}

        def w_dma():
            b = W["dma"]
            if b >= nblocks:
                return
            rel = [w_hi[b - RAW], w_lo[b - RAW]] if b >= RAW else []
            w_load[b] = sp.dma(wraw[:, b % RAW, :], wst[b], s_w[b % RAW], b // RAW + 1, rel)
            W["dma"] += 1

        def w_split():
            b = W["split"]
            if b >= nblocks:
                return
            rel = [w_pe[b - SPLIT]] if b >= SPLIT else []
            r, h, l = wraw[:, b % RAW, :], whi[:, b % SPLIT, :], wlo[:, b % SPLIT, :]
            w_hi[b] = fn(h, r, ACT.Copy, w_load[b], rel)
            w_lo[b] = tt(dve, l, r, h.bitcast(F32), ALU.subtract, w_hi[b], rel)
            W["split"] += 1

        s_m = [sem("s_m%d" % i) for i in range(2)]
        M = {"n": 0, "acc": [], "pe": []}
        m_tok = {}
        m_use = {}

        def mod_step():
            n = M["n"]
            if n >= 240:
                return
            v, k = n // 8, n % 8
            rel = m_use.get(n - 2, [])
            ld = sp.dma(mraw[:, n % 2, :], mst[n], s_m[n % 2], n // 2 + 1, rel)
            cc = SILU[:, k:k + 1] if v < 12 else SILU[:, 8 + k:9 + k]
            if k == 0:
                t = ts(dve, macc[:], mraw[:, n % 2, :], cc, None, ALU.mult, None, ld, t_silu, M["pe"])
            else:
                t = stt(macc[:], mraw[:, n % 2, :], cc, macc[:], ALU.mult, ALU.add, ld, M["acc"])
            m_use[n] = t
            M["acc"] = t
            M["n"] += 1
            if k == 7:
                i, b, rel = PB[0].get()
                for j in range(8):
                    last = mm(b[:, j:j + 1], macc[:, j * 128:(j + 1) * 128], C["ones"][:, 0:1], True, True,
                              rel, t, t_const["ones"], inc=(j == 7))
                bias = col("ada_b", 8 * v, 8) if v < 12 else col("b_mod", 8 * (v - 12), 8)
                m_tok[v] = tt(dve, MOD[:, v, :], b[:, 0:8], bias, ALU.add, last)
                M["pe"] = last
                bput(PB[0], i, m_tok[v])

        def mod_ready(v):
            while v not in m_tok:
                mod_step()
            return m_tok[v]

        def w_block_start(b):
            while W["dma"] < min(b + RAW, nblocks):
                w_dma()
                if b > 0:
                    break
            while W["split"] < min(b + SPLIT, nblocks):
                w_split()
            if b > 0:
                mod_step()

        def next_tiles(n, expect):
            t = W["tile"]
            b, o = t // BT, t % BT
            assert o + n <= BT
            assert [x[0] for x in tiles[t:t + n]] == expect, (tiles[t:t + n], expect)
            if o == 0:
                w_block_start(b)
            W["tile"] += n
            last = (o + n == BT) or W["tile"] == len(tiles)
            sl = slice(o * 128, (o + n) * 128)
            return b, whi[:, b % SPLIT, sl], wlo[:, b % SPLIT, sl], [w_hi[b], w_lo[b]], last

        def proj(nk, names, srch, srcl, ready, k0=0):
            got = [PB[0].get() for _ in names]
            ends = [None] * len(names)
            for k in range(nk):
                for m, name in enumerate(names):
                    b, wh, wl, w_ok, last = next_tiles(1, [name])
                    o = got[m][1]
                    waits = [w_ok, ready[k0 + k]] + ([got[m][2]] if k == 0 else [])
                    mm(o, wh, srch[:, k0 + k, :], k == 0, False, waits)
                    mm(o, wh, srcl[:, k0 + k, :], False, False)
                    fin = k == nk - 1
                    t = mm(o, wl, srch[:, k0 + k, :], False, fin, inc=last or fin)
                    if last:
                        w_pe[b] = t
                    if fin:
                        ends[m] = t
            return [(got[m][0], got[m][1], ends[m]) for m in range(len(names))]

        def proj_rows(nk, names, srch, srcl, ready):
            n = len(names)
            got = [PB[0].get() for _ in range(4)]
            ends = [None] * 4
            for k in range(nk):
                b, wh, wl, w_ok, last = next_tiles(n, names)
                for q in range(4):
                    o = got[q][1][:, 0:128 * n]
                    hs, ls = srch[:, k, q * 128:(q + 1) * 128], srcl[:, k, q * 128:(q + 1) * 128]
                    waits = [w_ok, ready[k]] + ([got[q][2]] if k == 0 else [])
                    mm(o, hs, wh, k == 0, False, waits)
                    mm(o, ls, wh, False, False)
                    fin = k == nk - 1
                    t = mm(o, hs, wl, False, fin, inc=(last and q == 3) or fin)
                    if fin:
                        ends[q] = t
                if last:
                    w_pe[b] = t
            return [(got[q][0], got[q][1], ends[q]) for q in range(4)]

        def rsqrt(ssb, n, waits, done):
            i0, m, r0 = T.get()
            i1, y, r1 = T.get()
            i2, a_, r2 = T.get()
            j, R, rr = RSR.get()
            t = ts(dve, m, ssb, 1.0 / n, EPS, ALU.mult, ALU.add, waits, r0)
            done(t)
            u = fn(y, m, ACT.Ln, t, r1)
            u = fn(y, y, ACT.Exp, u, scale=-0.5)
            t = stt(a_, y, -0.5, y, ALU.mult, ALU.mult, u, r2)
            t = tt(dve, a_, a_, m, ALU.mult, t)
            t = stt(R, a_, 1.5, y, ALU.add, ALU.mult, t, rr)
            T.put(i0, t)
            T.put(i1, t)
            T.put(i2, t)
            return j, R, t

        def set_table(name):
            act.do(lambda e: e.preload_act_table_set(name), inc=False)

        t_idr = cp(dve, identr[:], C["ident"][:], t_const["ident"])
        t_car = cp(dve, causr[:], C["caus"][:], t_const["caus"])
        t_bar = cp(dve, bandr[:], C["band"][:], t_const["band"])
        t_eps = None
        t_silu = fn(SILU[:], V[:, 0:16], ACT.Silu, t_vec)
        act.seen[t_vec[0]] = t_vec[2]
        lamc = col("lam", 0, 4)
        sm = small
        u = fn(sm[:, 0:4], lamc, ACT.Abs, t_vec)
        u = fn(sm[:, 0:4], sm[:, 0:4], ACT.Exp, u, scale=-1.0)
        u = fn(sm[:, 0:4], sm[:, 0:4], ACT.Ln, u, bias=1.0)
        t = ts(dve, sm[:, 4:8], lamc, -1.0, 0.0, ALU.mult, ALU.max, t_vec)
        t = tt(dve, sm[:, 4:8], sm[:, 4:8], sm[:, 0:4], ALU.add, t, u)
        t_cf = ts(dve, CF[:], sm[:, 4:8], -8.0, None, ALU.mult, None, t)
        t_qs = ts(dve, QS[:, 0:1], col("evq"), 0.125, None, ALU.mult, None, t_vec)
        t_qs = ts(dve, QS[:, 1:2], col("odq"), 0.125, None, ALU.mult, None, t_vec)

        PB[0] = banks(0, 1, 2, 3)
        OH = at("OH", ph, [33, 704])
        OHR = at("OHR", ph + 3584, [33, 704], F32R)
        TB = at("TB", ph + 7168, [33, 48])
        TBH = at("TBH", ph + 7424, [33, 48], F32R)
        TBL = at("TBL", ph + 7680, [33, 48], F32R)
        BI = at("BI", ph + 8192, [P, 16, 416])
        t_oh = sp.dma(OH[:], oh, s_c[2], 1)
        t_neg = pool.do(lambda e: e.memset(TB[32:33, :], NEG))
        t_tab = sp.dma(TB[0:32, :], tab, s_c[3], 1)
        t_ohr = cp(dve, OHR[:], OH[:], t_oh)
        t_tbh = cp(dve, TBH[:], TB[:], t_tab, t_neg)
        t_tbl = tt(dve, TBL[:], TB[:], TBH[:].bitcast(F32), ALU.subtract, t_tbh)
        for b in range(RAW):
            w_dma()

        def bias_tables():
            bb = banks(4, 5, 6, 7)
            toks = []
            for g, nk in ((0, 256), (1, 128), (2, 32)):
                for k0 in range(0, nk, 32):
                    i, b, rel = bb.get()
                    for k in range(k0, k0 + 32):
                        o = b[:, (k - k0) * 16:(k - k0 + 1) * 16]
                        if g == 2:
                            for j in range(4):
                                last = mm(o[32 * j:32 * j + 32, :], OH[:, 671 - k:703 - k], TB[:, 32:48], True, True,
                                          rel, t_oh, t_tab, t_neg, inc=(k == k0 + 31 and j == 3))
                            continue
                        l = OHR[:, 255 - k:383 - k] if g == 0 else OHR[:, 511 - k:639 - k]
                        mm(o, l, TBH[:, 16 * g:16 * g + 16], True, False, rel, t_ohr, t_tbl)
                        last = mm(o, l, TBL[:, 16 * g:16 * g + 16], False, True, inc=(k == k0 + 31))
                    base_ = (0, 256, 384)[g] + k0
                    dst = BI[:, :, base_:base_ + 32]
                    src = b.rearrange("p (k h) -> p h k", h=16)
                    if (k0 // 32) % 2 == 0:
                        t = fn(dst, src, ACT.Copy, last)
                    else:
                        t = cp(dve, dst, src, last)
                    toks.append(t)
                    bput(bb, i, t)
                    yield
            B["stored"] = sp.dma(scratch, BI[:], s_c[4], 1, toks)

        B = {}

        x_tok = [t_x] * 8
        hs_pe = []

        def sq_add(m, src, tok, first, st):
            if first:
                u = fn(SQ[:], src, ACT.Square, tok, st["free"])
                st["sq"] = u
                return
            i, b, rel = T.get()
            u = fn(b, src, ACT.Square, tok, rel)
            st["sq"] = tt(dve, SQ[:], SQ[:], b, ALU.add, u, st["sq"])
            T.put(i, st["sq"])

        SQS = {"free": [], "sq": None}

        def total(st, n):
            i, b, rel = PB[0].get()
            t = mm(b, C["ones"][:], SQ[:], True, True, rel, st["sq"], t_const["ones"], inc=True)
            st["free"] = t
            return rsqrt(b, n, t, lambda tk: bput(PB[0], i, tk))

        def modulate(shift, amul, t_mod):
            j, R, tr = total(SQS, 1024)
            toks = []
            for m in range(8):
                i, b, rel = T.get()
                t = stt(b, X[:, m, :], amul[:, m:m + 1], R, ALU.mult, ALU.mult, tr, x_tok[m], t_mod, rel)
                u = fn(HH[:, m, :], b, ACT.Identity, t, t_mod, hs_pe[0], bias=shift[:, m:m + 1])
                v = stt(HL[:, m, :], b, shift[:, m:m + 1], HH[:, m, :].bitcast(F32), ALU.add, ALU.subtract, u, hs_pe[0])
                T.put(i, v)
                toks.append([u, v])
            RSR.put(j, t)
            return toks

        hs_pe.append([])

        def amul(idx, v, gain):
            t = mod_ready(v)
            return stt(AM[:, idx, :], MOD[:, v, :], 1.0, gain, ALU.add, ALU.mult, t, t_vec)

        def residual(m, pb, gate, t_gate, last_q):
            i, b, t = pb
            u = stt(X[:, m, :], b, gate[:, m:m + 1], X[:, m, :], ALU.mult, ALU.add, t, t_gate, x_tok[m])
            bput(PB[0], i, u)
            x_tok[m] = u
            return u

        def split_out(dh, dl, src, waits):
            u = fn(dh, src, ACT.Copy, waits)
            v = tt(dve, dl, src, dh.bitcast(F32), ALU.subtract, u)
            return [u, v]

        def ffn(tag, ready, conv, sink):
            PH = at("PH" + tag, ph, [P, 11, S], F32R)
            PL = at("PL" + tag, ph + 22528, [P, 11, S], F32R)
            PB[0] = banks(0, 1, 2, 3, 4, 5, 6, 7)
            down = [[], []]
            set_table("silu_and_others")

            def product(i, half, g, u):
                gi, gb, gt = g
                ui, ub, ut = u
                k = i - 11 * half
                i0, a_, r0 = T.get()
                if conv is not None:
                    cw, cb = cols["fcw"][0] + 66 * conv, cols["fcb"][0] + 22 * conv
                    w = lambda j: V[:, cw + 22 * j + i:cw + 22 * j + i + 1]
                    i1, y, r1 = T.get()
                    t = fn(y, gb, ACT.Identity, gt, r1, bias=V[:, cb + i:cb + i + 1], scale=w(2))
                    t = stt(y[:, 1:S], gb[:, 0:S - 1], w(1), y[:, 1:S], ALU.mult, ALU.add, t)
                    t = stt(y[:, 2:S], gb[:, 0:S - 2], w(0), y[:, 2:S], ALU.mult, ALU.add, t)
                    bput(PB[0], gi, t)
                    t = fn(a_, y, ACT.Silu, t, r0)
                    T.put(i1, t)
                else:
                    t = fn(a_, gb, ACT.Silu, gt, r0)
                    bput(PB[0], gi, t)
                t = tt(dve, a_, a_, ub, ALU.mult, t, ut)
                bput(PB[0], ui, t)
                r = split_out(PH[:, k, :], PL[:, k, :], a_, [t, down[0]])
                T.put(i0, r[1])
                return r

            for half in (0, 1):
                ok = [None] * 11
                i = 11 * half
                if half == 0:
                    ps_ = proj(8, [tag + "g", tag + "u"] * 2, HH, HL, ready)
                    for z in range(2):
                        ok[z] = product(z, 0, ps_[2 * z], ps_[2 * z + 1])
                    i = 2
                while i < 11 * half + 11:
                    ps_ = proj(8, [tag + "g", tag + "u"], HH, HL, ready)
                    ok[i - 11 * half] = product(i, half, ps_[0], ps_[1])
                    i += 1
                if half == 1:
                    hs_pe[0] = [ps_[1][2]]
                for m in range(8):
                    r = proj(11, [tag + "d%d" % half], PH, PL, ok)
                    sink(half, m, r[0])
                    down[0] = [r[0][2]]
            set_table("natural_log_exp_and_others")

        def phase_free():
            return phase_tok

        phase_tok = []

        def body():
            for m in range(8):
                sq_add(m, X[:, m, :], x_tok[m], m == 0, SQS)

            g_bias = bias_tables()
            next(g_bias)
            for _ in range(16):
                mod_step()
                next(g_bias, None)
            for _ in g_bias:
                pass
            set_table("natural_log_exp_and_others")

            def first_norm(layer, which, idx):
                v = 6 * layer + 3 * which
                gain = col(("mix_g", "ffn_g")[which], 8 * layer, 8)
                t = amul(idx, v + 1, gain)
                t2 = mod_ready(v)
                return modulate(MOD[:, v, :], AM[:, idx, :], [t, t2])

            def qk_norm(pb, g, dst, gt, n=64):
                i, b, t = pb
                i0, q, r0 = T.get()
                u = fn(q, b, ACT.Square, t, r0)
                j, sb_, rel = QB[0].get()
                w = mm(sb_, C["blk"][:], q, True, True, rel, u, t_const["blk"], inc=True)
                T.put(i0, w)
                k, R, tr = rsqrt(sb_, n, w, lambda tk: bput(QB[0], j, tk))
                t = stt(dst, b, g, R, ALU.mult, ALU.mult, tr, gt)
                RSR.put(k, t)
                bput(PB[0], i, t)
                return t

            QB = [None]

            h_ok = first_norm(0, 0, 0)
            PB[0] = banks(0, 1, 2, 3, 4, 5)
            LB = banks(6, 7)
            QB[0] = LB
            YH = at("YH", ph, [P, 4, S], F32R)
            YL = at("YL", ph + 8192, [P, 4, S], F32R)
            Q = at("Q", ph + 16384, [P, 4, S])
            K = at("K", ph + 24576, [P, 4, S])
            VV = at("VV", ph + 32768, [P, 4, S])
            XC = at("XC", ph + 40960, [P, 4, S])
            RR = at("RR", ph + 49152, [P, 4, S])
            GI = at("GI", ph + 57344, [P, 4, S])
            GE = at("GE", ph + 65536, [P, 4, S])
            WAX = at("WAX", ph + 73728, [P, 8, 128])
            t_bi = B["stored"]
            t_wax = sp.dma(WAX[:], wax, s_c[5], 1, t_bi)
            xr, gr = {}, {}
            a_ps = proj(8, ["ev_in"] * 4, HH, HL, h_ok)
            xr[0], gr[0], xr[1], gr[1] = a_ps
            st = {"r": {}, "gi": {}, "ge": {}, "T": {}, "a": {}}

            def lru_front(m):
                i, b, t = xr[m]
                w = lambda j: col("cw", 4 * j + m)
                u = fn(XC[:, m, :], b, ACT.Identity, t, t_bi, bias=col("cb", m), scale=w(3))
                for s_, j in ((1, 2), (2, 1), (3, 0)):
                    u = stt(XC[:, m, s_:S], b[:, 0:S - s_], w(j), XC[:, m, s_:S], ALU.mult, ALU.add, u)
                bput(PB[0], i, u)
                t_xc = u
                i, b, t = gr[m]
                i0, z, r0 = T.get()
                u = fn(z, b, ACT.Square, t, r0)
                u = ts(dve, z, z, 0.044715, 1.0, ALU.mult, ALU.add, u)
                u = tt(dve, z, z, b, ALU.mult, u)
                u = fn(z, z, ACT.Tanh, u, scale=math.sqrt(2.0 / math.pi))
                u = stt(GE[:, m, :], z, 1.0, b, ALU.add, ALU.mult, u, t_bi)
                st["ge"][m] = u
                T.put(i0, u)
                bput(PB[0], i, u)
                yield
                j0, b0, rel0 = LB.get()
                v0 = mm(b0, WAX[:, m, :], XC[:, m, :], True, True, rel0, t_xc, t_wax, inc=True)
                j1, b1, rel1 = LB.get()
                v1 = mm(b1, WAX[:, 4 + m, :], XC[:, m, :], True, True, rel1, inc=True)
                yield
                u0 = fn(RR[:, m, :], b0, ACT.Sigmoid, v0, t_bi, bias=col("ba", m))
                bput(LB, j0, u0)
                i0, z, r0 = T.get()
                u1 = fn(z, b1, ACT.Sigmoid, v1, r0, bias=col("bx", m))
                bput(LB, j1, u1)
                t = tt(dve, GI[:, m, :], z, XC[:, m, :], ALU.mult, u1, t_bi)
                T.put(i0, t)
                st["gi"][m] = t
                st["T"][m] = fn(XC[:, m, :], RR[:, m, :], ACT.Tanh, u0, t, t_cf, scale=CF[:, m:m + 1])

            def lru_back(m):
                u = fn(RR[:, m, :], RR[:, m, :], ACT.Exp, st["T"][m], scale=CF[:, m:m + 1])
                st["a"][m] = u

            def lru_end(m):
                i0, z, r0 = T.get()
                i1, y, r1 = T.get()
                t = ts(dve, z, XC[:, m, :], -1.0, 1.0, ALU.mult, ALU.add, st["T"][m], r0)
                t = recip(z, z, t)
                t = stt(z, XC[:, m, :], -2.0, z, ALU.mult, ALU.mult, t)
                u = fn(z, z, ACT.Sqrt, t)
                t = tt(dve, z, z, GI[:, m, :], ALU.mult, u)
                t = dve.do(lambda e: e.tensor_tensor_scan(y, RR[:, m, :], z, 0.0, ALU.mult, ALU.add), t, st["a"][m], r1)
                T.put(i0, t)
                t = stt(y, y, 0.5, GE[:, m, :], ALU.mult, ALU.mult, t)
                r = split_out(YH[:, m, :], YL[:, m, :], y, [t, t_bi])
                T.put(i1, r[1])
                ya_ok[m] = r

            ya_ok = {}

            def lru_all():
                for m in range(4):
                    yield from lru_front(m)
                    yield
                for m in range(4):
                    lru_back(m)
                yield
                for m in range(4):
                    lru_end(m)
                    yield

            q_tok, k_tok, v_tok = {}, {}, {}

            def even_rest():
                vs = proj_rows(8, ["ev_in"] * 4, HH, HL, h_ok)
                for q, (i, b, t) in enumerate(vs):
                    u = fn(VV[:, q, :], b, ACT.Copy, t, t_bi)
                    v_tok[q] = u
                    bput(PB[0], i, u)
                yield

            lf0 = lru_front(0)
            next(lf0)
            lf1 = lru_front(1)
            next(lf1)
            b_ps = proj(8, ["ev_in"] * 4, HH, HL, h_ok)
            xr[2], gr[2], xr[3], gr[3] = b_ps
            for z in (lf0, lf1):
                for _ in z:
                    pass
            lf2, lf3 = lru_front(2), lru_front(3)
            next(lf2)
            next(lf3)
            for _ in even_rest():
                pass
            for z in (lf2, lf3):
                for _ in z:
                    pass
            for m in range(4):
                lru_back(m)
            for m in range(4):
                lru_end(m)
            set_table("natural_log_exp_and_others")
            for m in range(8):
                r = proj(8, ["ev_in"], HH, HL, h_ok)[0]
                if m == 7:
                    hs_pe[0] = [r[2]]
                if m > 0:
                    prev()
                prev = (lambda r=r, m=m: q_tok.__setitem__(m, qk_norm(r, QS[:, 0:1], Q[:, m, :], [t_qs, t_bi]))) if m < 4 else \
                    (lambda r=r, m=m: k_tok.__setitem__(m - 4, qk_norm(r, col("evk"), K[:, m - 4, :], [t_vec, t_bi])))
            prev()

            ZB, VB, OB = banks(0, 1, 2, 3), banks(4, 5), banks(6, 7)
            lru_done = [ya_ok[m] for m in range(4)]
            SPB = Ring([at("SPB%d" % i, ph + 40960 + 10240 * i, [P, 1280]) for i in range(3)])
            SNB = Ring([at("SNB%d" % i, ph + 40960 + 10240 * i + 5120, [P, 1280]) for i in range(3)])
            off = [0, 512, 896, 1152]
            wid = [512, 384, 256, 128]
            y_ok = dict(ya_ok)
            ob = {}

            def stick_front(h):
                half = 64 * (h % 2)
                i1, sp_, r1 = SPB.get()
                i2, sn_, r2 = SNB.get()
                toks = {}
                for kt in (3, 2, 1, 0):
                    n, o = wid[kt], off[kt]
                    i, b, rel = ZB.get()
                    z = b[:, 0:n]
                    t = mm(z, K[half:half + 64, h // 2, kt * 128:(kt + 1) * 128], Q[half:half + 64, h // 2, S - n:S],
                           True, True, rel, q_tok[h // 2], k_tok[h // 2], inc=True)
                    i0, l, r0 = T.get()
                    l = l[:, 0:n]
                    u = fn(l, z, ACT.Abs, t, r0)
                    u = fn(l, l, ACT.Exp, u, scale=-1.0)
                    u = fn(l, l, ACT.Ln, u, bias=1.0)
                    a1 = stt(sp_[:, o:o + n], z, 0.0, l, ALU.max, ALU.add, u, r1, lru_done)
                    a2 = stt(sn_[:, o:o + n], z, 0.0, l, ALU.min, ALU.subtract, r2)
                    bput(ZB, i, a2)
                    T.put(i0, a2)
                    a1 = tt(pool, sp_[:, o:o + 128], sp_[:, o:o + 128], C["tri"][:], ALU.mult, a1, t_const["tri"])
                    toks[kt] = (a1, a2)
                return i1, sp_, i2, sn_, toks

            def stick_back(h, fr):
                i1, sp_, i2, sn_, toks = fr
                half = 64 * (h % 2)
                w_t = {}
                for kt in (3, 2, 1, 0):
                    n, o = wid[kt], off[kt]
                    i, b, rel = VB.get()
                    last = mm(b[:, 0:n], C["later"][:], sp_[:, o:o + n], True, kt == 3, rel, toks[kt], t_const["later"],
                              inc=(kt == 3))
                    for k2 in range(kt + 1, 4):
                        n2, o2 = wid[k2], off[k2]
                        last = mm(b[:, n - n2:n], C["ones"][:], sp_[:, o2:o2 + n2], False, k2 == 3, toks[k2],
                                  inc=(k2 == 3))
                    w = sn_[:, o:o + n]
                    t = tt(dve, w, w, b[:, 0:n], ALU.subtract, last, toks[kt])
                    bput(VB, i, t)
                    u = fn(w, w, ACT.Exp, t)
                    v = tt(pool, sn_[:, o:o + 128], sn_[:, o:o + 128], C["tri"][:], ALU.mult, u)
                    w_t[kt] = [u, v]
                    sp_last = last
                SPB.put(i1, sp_last)
                if h % 2 == 0:
                    ob[h // 2] = OB.get()
                j, b, rel = ob[h // 2]
                for kt in range(4):
                    n, o = wid[kt], off[kt]
                    t = mm(b[half:half + 64, S - n:S], VV[:, kt, 64 * h:64 * h + 64], sn_[:, o:o + n], kt == 0, kt == 3,
                           rel, w_t[kt], v_tok[kt], inc=(kt == 3))
                SNB.put(i2, t)
                if h % 2 == 1:
                    m = 4 + h // 2
                    r = split_out(HH[:, m, :], HL[:, m, :], b, [t, hs_pe[0]])
                    bput(OB, j, r)
                    y_ok[m] = r

            fr = stick_front(0)
            for h in range(8):
                nx = stick_front(h + 1) if h < 7 else None
                stick_back(h, fr)
                fr = nx

            def out_proj(name, ready, gate, t_gate, srcs):
                SQS["sq"] = None
                for m in range(8):
                    got = [PB[0].get()]
                    for k in range(8):
                        b, wh, wl, w_ok, last = next_tiles(1, [name])
                        o = got[0][1]
                        sh, sl, kk = srcs(k)
                        waits = [w_ok, ready[k]] + ([got[0][2]] if k == 0 else [])
                        mm(o, wh, sh[:, kk, :], k == 0, False, waits)
                        mm(o, wh, sl[:, kk, :], False, False)
                        t = mm(o, wl, sh[:, kk, :], False, k == 7, inc=last or k == 7)
                        if last:
                            w_pe[b] = t
                    sink = gate(m, (got[0][0], o, t))
                hs_pe[0] = [t]
                return t

            def add_gated(v):
                tg = mod_ready(v)

                def sink(m, pb):
                    u = residual(m, pb, MOD[:, v, :], tg, None)
                    sq_add(m, X[:, m, :], u, m == 0, SQS)
                return sink

            PB[0] = banks(0, 1, 2, 3, 4, 5, 6, 7)
            t_ph = out_proj("ev_out", y_ok, add_gated(2), None,
                            lambda k: (YH, YL, k) if k < 4 else (HH, HL, k))
            phase_tok[:] = [t_ph]

            def guard():
                for q in (act, dve, pool, sp):
                    for w in flat(phase_tok):
                        q.ops.append(([(w[1], w[2])] if q.seen.get(w[0], 0) < w[2] else [], None, 0))
                        q.seen[w[0]] = max(q.seen.get(w[0], 0), w[2])

            guard()

            def first_ffn(layer):
                ready = first_norm(layer, 1, 2 * layer + 1)
                v = 6 * layer + 5
                tg = mod_ready(v)

                def sink(half, m, pb):
                    u = residual(m, pb, MOD[:, v, :], tg, None)
                    if half == 1:
                        sq_add(m, X[:, m, :], u, m == 0, SQS)
                        phase_tok[:] = [pb[2]]
                ffn("f%d" % layer, ready, layer, sink)
                guard()

            first_ffn(0)

            h_ok = first_norm(1, 0, 2)
            PB[0] = banks(0, 1, 2, 3, 4, 5)
            QB[0] = banks(6, 7)
            Q2 = at("Q2", ph, [P, 8, S])
            K2 = at("K2", ph + 16384, [P, 2, S])
            V2 = at("V2", ph + 20480, [P, 4, 256])
            PP = Ring([at("PP%d" % i, ph + 24576 + 4096 * i, [P, 4, 256]) for i in range(3)])
            PTS = Ring([at("PTS%d" % i, ph + 36864 + 4096 * i, [P, 2, 512]) for i in range(3)])
            q_tok, k_tok, v_tok = {}, {}, {}
            pend = []

            def odd_sink(m, r):
                if m < 8:
                    q_tok[m] = qk_norm(r, QS[:, 1:2], Q2[:, m, :], t_qs)
                else:
                    k_tok[m - 8] = qk_norm(r, col("odk"), K2[:, m - 8, :], t_vec)

            for m, r in enumerate(proj(8, ["od_in"] * 4, HH, HL, h_ok)):
                pend.append((m, r))
            for m in range(4, 10):
                r = proj(8, ["od_in"], HH, HL, h_ok)[0]
                pend.append((m, r))
                while len(pend) > (4 if m < 7 else 1):
                    odd_sink(*pend.pop(0))
            while pend:
                odd_sink(*pend.pop(0))
            vs = proj_rows(8, ["od_in"] * 2, HH, HL, h_ok)
            hs_pe[0] = [vs[3][2]]
            for q, (i, b, t) in enumerate(vs):
                u = fn(V2[:, q, :], b[:, 0:256], ACT.Copy, t)
                v_tok[q] = u
                bput(PB[0], i, u)

            SB2 = Ring([ps[:, 0:2, :], ps[:, 2:4, :]])
            SB2.rel = [[bankrel[0], bankrel[1]], [bankrel[2], bankrel[3]]]
            PTB = banks(4, 5)
            OB = banks(6, 7)
            smr = Ring([small[:, 16 * i:16 * i + 16] for i in range(4)])
            y_ok = {m: [] for m in range(8)}
            ob = {}

            def swa_front(n, g):
                half = 64 * (g % 2)
                c0 = 0 if n else 1
                i, b, rel = SB2.get()
                sc = b.rearrange("p a (h k) -> p (a h) k", h=2)
                kk = K2[half:half + 64, g // 2, (n - 1 + c0) * 128:(n + 1) * 128]
                for j in range(4):
                    o = sc[:, j, 128 * c0:256]
                    mm(o, Q2[half:half + 64, 4 * (g // 2) + j, n * 128:(n + 1) * 128], kk, True, False,
                       rel, q_tok[4 * (g // 2) + j], k_tok[g // 2])
                    t = mm(o, identr[:], bandr[:, 128 * c0:256], False, True, t_idr, t_bar, inc=(j == 3))
                si, s_, sr = smr.get()
                u = dve.do(lambda e: e.tensor_reduce(s_[:, 0:4], sc[:, :, 128 * c0:256], AX.X, ALU.max), t, sr)
                sk = col("sinks", 4 * g, 4)
                u = tt(dve, s_[:, 0:4], s_[:, 0:4], sk, ALU.max, u)
                t1 = tt(dve, s_[:, 4:8], sk, s_[:, 0:4], ALU.subtract, u)
                u = ts(dve, s_[:, 0:4], s_[:, 0:4], -1.0, None, ALU.mult, None, t1)
                e1 = fn(s_[:, 8:12], s_[:, 4:8], ACT.Exp, t1)
                pi, pp, pr = PP.get()
                for j in range(4):
                    v = fn(pp[:, j, 128 * c0:256], sc[:, j, 128 * c0:256], ACT.Exp, u, pr,
                           bias=s_[:, j:j + 1], acc=s_[:, 12 + j:13 + j])
                SB2.put(i, v)
                for q in range(2):
                    bankrel[2 * i + q] = [v]
                w = tt(dve, s_[:, 12:16], s_[:, 12:16], s_[:, 8:12], ALU.add, v, e1)
                w = recip(s_[:, 12:16], s_[:, 12:16], w)
                for j in range(4):
                    w2 = ts(dve, pp[:, j, 128 * c0:256], pp[:, j, 128 * c0:256], s_[:, 12 + j:13 + j], None, ALU.mult, None, w)
                smr.put(si, w2)
                return n, g, c0, pi, pp, w2

            def swa_back(f):
                n, g, c0, pi, pp, tok = f
                half = 64 * (g % 2)
                xi, px, xr_ = PTS.get()
                cps = {}
                for c in range(c0, 2):
                    i, b, rel = PTB.get()
                    for j in range(4):
                        t = tpose(b[:, j * 128:(j + 1) * 128], pp[:, j, c * 128:(c + 1) * 128], C["ident"][:],
                                  rel, tok, t_const["ident"], inc=(j == 3))
                    cps[c] = fn(px[:, c, :], b, ACT.Copy, t, xr_) if c == 0 else cp(dve, px[:, c, :], b, t, xr_)
                    bput(PTB, i, cps[c])
                PP.put(pi, t)
                key = (n, g // 2)
                if g % 2 == 0:
                    ob[key] = OB.get()
                j, b, rel = ob[key]
                for c in range(c0, 2):
                    t = mm(b[half:half + 64, :], V2[:, n - 1 + c, 64 * g:64 * g + 64], px[:, c, :], c == c0, c == 1,
                           rel, cps[c], v_tok[n - 1 + c], inc=(c == 1))
                PTS.put(xi, t)
                if g % 2 == 1:
                    a_ = 4 * (g // 2)
                    src = b.rearrange("p (j q) -> p j q", j=4)
                    r = split_out(HH[:, a_:a_ + 4, n * 128:(n + 1) * 128], HL[:, a_:a_ + 4, n * 128:(n + 1) * 128],
                                  src, [t, hs_pe[0]])
                    bput(OB, j, r)
                    for m in range(a_, a_ + 4):
                        y_ok[m].append(r)

            units = [(n, g) for n in range(4) for g in range(4)]
            fr = [swa_front(*units[0])]
            for x_ in units[1:]:
                fr.append(swa_front(*x_))
                swa_back(fr.pop(0))
            swa_back(fr.pop(0))
            PB[0] = banks(0, 1, 2, 3, 4, 5, 6, 7)
            t_ph = out_proj("od_out", y_ok, add_gated(8), None, lambda k: (HH, HL, k))
            phase_tok[:] = [t_ph]
            guard()
            first_ffn(1)

            def pre_norm(layer, sub):
                v = 12 + 9 * layer + 3 * sub
                idx = 4 + 3 * layer + sub
                t = amul(idx, v + 1, col("pre", 24 * layer + 8 * sub, 8))
                t2 = mod_ready(v)
                return modulate(MOD[:, v, :], AM[:, idx, :], [t, t2])

            YS = {"tok": [None] * 8}

            def y_store(Y, m, pb, half, st2):
                i, b, t = pb
                if half == 0:
                    u = fn(Y[:, m, :], b, ACT.Copy, t)
                    YS["tok"][m] = u
                    bput(PB[0], i, u)
                    return
                if half == 1:
                    u = tt(dve, Y[:, m, :], b, Y[:, m, :], ALU.add, t, YS["tok"][m])
                else:
                    u = cp(dve, Y[:, m, :], b, t)
                YS["tok"][m] = u
                bput(PB[0], i, u)
                sq_add(m, Y[:, m, :], u, m == 0, SQS)

            def post_norm(Y, layer, sub, last=False):
                v = 12 + 9 * layer + 3 * sub + 2
                idx = 3 * layer + sub
                tg = mod_ready(v)
                t0 = stt(GM[:, idx, :], MOD[:, v, :], (0.5, 1.0, 0.5)[sub], col("post", 24 * layer + 8 * sub, 8),
                         ALU.mult, ALU.mult, tg, t_vec)
                j, R, tr = total(SQS, 1024)
                for m in range(8):
                    t = stt(Y[:, m, :], Y[:, m, :], GM[:, idx, m:m + 1], R, ALU.mult, ALU.mult, tr, t0, YS["tok"][m], SQS["sq"])
                    t = tt(dve, X[:, m, :], X[:, m, :], Y[:, m, :], ALU.add, t, x_tok[m])
                    x_tok[m] = t
                    if not last:
                        sq_add(m, X[:, m, :], t, m == 0, SQS)
                RSR.put(j, t)
                phase_tok[:] = [t]
                guard()

            def second_ffn(layer, which):
                sub = 2 * which
                ready = pre_norm(layer, sub)
                tag = "ab"[layer] + str(which)
                Y = at("Y" + tag, ph + 45056, [P, 8, S])
                ffn(tag, ready, None, lambda half, m, pb: y_store(Y, m, pb, half, None))
                post_norm(Y, layer, sub, last=(layer == 1 and which == 1))

            second_ffn(0, 0)

            h_ok = pre_norm(0, 1)
            PB[0] = banks(0, 1, 2, 3, 4, 5)
            CL = at("CL", ph, [P, 5, S])
            CH = at("CH", ph + 10240, [P, 5, S], F32R)
            CW = at("CW", ph + 20480, [P, 5, S], F32R)
            VM = at("VM", ph + 30720, [P, 4, 1024])
            TG = at("TG", ph + 47104, [P, S])
            KRP = at("KRP", ph + 49152, [P, S])
            QH = Ring([at("QH%d" % i, ph + 51200 + 2048 * i, [P, S]) for i in range(3)])
            KH = Ring([at("KH%d" % i, ph + 57344 + 2048 * i, [P, S]) for i in range(3)])
            PM = Ring([at("PM%d" % i, ph + 63488 + 2048 * i, [P, S]) for i in range(4)])
            PTM = Ring([at("PTM%d" % i, ph + 71680 + 2048 * i, [P, S]) for i in range(3)])
            t_trig = sp.dma(TG[:], trig, s_c[6], 1)
            lat = proj(8, ["mla_in"] * 6, HH, HL, h_ok)
            hs_pe[0] = [lat[5][2]]
            SBQ = banks(6, 7)

            def lat_norm(tiles_, n, gname, out0):
                i, b, rel = SBQ.get()
                cpt = []
                for k, m in enumerate(tiles_):
                    bi, bk, bt = lat[m]
                    i0, z, r0 = T.get()
                    u = fn(z, bk, ACT.Square, bt, r0)
                    w = mm(b, C["ones"][:], z, k == 0, k == len(tiles_) - 1, rel, u, inc=True)
                    T.put(i0, w)
                    c = cp(dve, CL[:, m, :], bk, bt, u)
                    bput(PB[0], bi, c, u)
                    cpt.append(c)
                j, R, tr = rsqrt(b, n, w, lambda tk: bput(SBQ, i, tk))
                for k, m in enumerate(tiles_):
                    t = stt(CL[:, m, :], CL[:, m, :], col(gname, k), R, ALU.mult, ALU.mult, tr, cpt[k])
                    c_ok[m] = split_out(CH[:, m, :], CW[:, m, :], CL[:, m, :], t)
                RSR.put(j, t)

            c_ok = {}
            lat_norm([3, 4], 256, "mkv", 3)
            lat_norm([0, 1, 2], 384, "mq", 0)

            def rope(dst, b, t, extra):
                i0, z, r0 = T.get()
                t1 = tt(dve, dst, b[64:96, :], TG[64:96, :], ALU.mult, t, t_trig, extra)
                t2 = tt(dve, z[64:96, :], b[96:128, :], TG[96:128, :], ALU.mult, t, r0)
                t3 = tt(pool, dst, dst, z[64:96, :], ALU.add, t1, t2)
                T.put(i0, t3)
                return t3, t2

            bi, bk, bt = lat[5]
            t_kr, tb_ = rope(KRP[64:96, :], bk, bt, [])
            bput(PB[0], bi, tb_)
            vm_tok = {}
            for f in range(2):
                vs = proj_rows(2, ["mla_v"] * 4, CH[:, 3:5, :], CW[:, 3:5, :], {0: c_ok[3], 1: c_ok[4]})
                for q, (i, b, t) in enumerate(vs):
                    u = fn(VM[:, q, 512 * f:512 * f + 512], b, ACT.Copy, t)
                    vm_tok[(q, f)] = u
                    bput(PB[0], i, u)
            PB[0] = banks(6, 7)
            SM = banks(0, 1, 2)
            PTB = banks(3, 4)
            OB = banks(5)
            MH = {}
            kbank = {}

            def mla_proj(h):
                i, b, t = proj(3, ["mla_q"], CH, CW, c_ok)[0]
                qi, q, qr = QH.get()
                u1 = fn(q[0:64, :], b[0:64, :], ACT.Copy, t, qr)
                u2, u3 = rope(q[64:96, :], b, t, qr)
                bput(PB[0], i, u1, u3)
                yield
                if h % 2 == 0:
                    i, b, t = proj(2, ["mla_k"], CH, CW, c_ok, k0=3)[0]
                    kt_ = []
                    for z in range(2):
                        ki, k, kr = KH.get()
                        w1 = fn(k[0:64, :], b[64 * z:64 * z + 64, :], ACT.Copy, t, kr)
                        w2 = pool.do(lambda e, k=k: e.tensor_copy(k[64:96, :], KRP[64:96, :]), t_kr, kr)
                        kbank[h + z] = (ki, k, [w1, w2])
                    bput(PB[0], i, w1)
                MH[h] = (qi, q, [u1, u2]) + kbank[h]
                yield

            def mla_att(h):
                qi, q, qt, ki, k, kt_ = MH[h]
                half = 64 * (h % 2)
                if h % 2 == 0:
                    ob["m"] = OB.get()
                j, ob_, orel = ob["m"]
                fronts = []

                def front(n):
                    w = 128 * (n + 1)
                    i, b, rel = SM.get()
                    mm(b[:, 0:w], q[0:96, n * 128:(n + 1) * 128], k[0:96, 0:w], True, False, rel, qt, kt_)
                    t = mm(b[:, w - 128:w], identr[:], causr[:], False, True, t_idr, t_car, inc=True)
                    si, s_, sr = smr.get()
                    u = dve.do(lambda e: e.tensor_reduce(s_[:, 0:1], b[:, 0:w], AX.X, ALU.max), t, sr)
                    u = ts(dve, s_[:, 0:1], s_[:, 0:1], -MLA_SCALE, None, ALU.mult, None, u)
                    pi, pp, pr = PM.get()
                    v = fn(pp[:, 0:w], b[:, 0:w], ACT.Exp, u, pr, bias=s_[:, 0:1], scale=MLA_SCALE, acc=s_[:, 1:2])
                    bput(SM, i, v)
                    x_ = recip(s_[:, 1:2], s_[:, 1:2], v)
                    x_ = ts(dve, pp[:, 0:w], pp[:, 0:w], s_[:, 1:2], None, ALU.mult, None, x_)
                    smr.put(si, x_)
                    return n, pi, pp, x_, t

                def back(n, pi, pp, tok):
                    w = 128 * (n + 1)
                    i, b, rel = PTB.get()
                    for c in range(n + 1):
                        t = tpose(b[:, c * 128:(c + 1) * 128], pp[:, c * 128:(c + 1) * 128], C["ident"][:], rel, tok,
                                  inc=(c == n))
                    PM.put(pi, t)
                    xi, px, xr_ = PTM.get()
                    u = fn(px[:, 0:w], b[:, 0:w], ACT.Copy, t, xr_) if n % 2 else cp(dve, px[:, 0:w], b[:, 0:w], t, xr_)
                    bput(PTB, i, u)
                    for c in range(n + 1):
                        t = mm(ob_[half:half + 64, n * 128:(n + 1) * 128], VM[:, c, 64 * h:64 * h + 64],
                               px[:, c * 128:(c + 1) * 128], c == 0, c == n, orel, u, vm_tok[(c, h // 8)], inc=(c == n))
                    PTM.put(xi, t)
                    return t

                fr_ = None
                for n in (0, 1, 2, 3):
                    f = front(n)
                    if n == 3:
                        QH.put(qi, f[4])
                        KH.put(ki, f[4])
                    if fr_ is not None:
                        back(*fr_[:4])
                    fr_ = f
                    yield
                t = back(*fr_[:4])
                if h % 2 == 1:
                    m = h // 2
                    r = split_out(HH[:, m, :], HL[:, m, :], ob_, [t, hs_pe[0]])
                    bput(OB, j, r)
                    y_ok[m] = r
                yield

            y_ok = {}
            for _ in mla_proj(0):
                pass
            for h in range(16):
                if h < 15:
                    weave(mla_att(h), mla_proj(h + 1), 2)
                else:
                    for _ in mla_att(h):
                        pass
            PB[0] = banks(0, 1, 2, 3, 4, 5, 6, 7)
            phase_tok[:] = [y_ok[7]]
            guard()
            Y = at("Ymla", ph + 45056, [P, 8, S])
            t_ph = out_proj("mla_o", y_ok, lambda m, pb: y_store(Y, m, pb, 2, None), None, lambda k: (HH, HL, k))
            post_norm(Y, 0, 1)
            second_ffn(0, 1)
            second_ffn(1, 0)

            h_ok = pre_norm(1, 1)
            for _ in range(240):
                mod_step()
            mod_done = [m_tok[29], m_use[239]]
            PB[0] = banks(4, 5, 6, 7)
            YF = at("YF", ph, [P, 8, S])
            QK = Ring([at("QK%d" % i, ph + 16384 + 12288 * i, [P, 6, S]) for i in range(2)])
            VT = at("VT", ph + 40960, [P, 3, S])
            VN = Ring([at("VN%d" % i, ph + 47104 + 6144 * i, [P, 12, 128]) for i in range(2)])
            SD = Ring([at("SD%d" % i, ph + 59392 + 6144 * i, [P, 1536]) for i in range(2)])
            PD = at("PD", ph + 71680, [P, 1408])
            BB = Ring([at("BB%d" % i, macc_off - 8192 + 4096 * i, [P, 2, 416]) for i in range(2)])
            RB = at("RB", macc_off, [P, 4, 4, 32])
            s_bb = [sem("s_bb%d" % i) for i in range(2)]
            mrow = at("mrow", macc_off + 2048, [2, S])
            vt_rel, dl = [[]], {}
            pool_b = banks(0, 1, 2, 3)
            first4 = proj(8, ["dil_in"] * 4, HH, HL, h_ok)
            for i_ in range(4):
                pass

            def tok_view(ap, g, j):
                if g == 0:
                    return ap[:, 128 * j:128 * j + 128]
                if g == 1:
                    return ap.rearrange("p (i r) -> p r i", r=4)[:, j, :]
                return ap.rearrange("p (k a j) -> p j a k", k=32, a=4)[:, j, :, :]

            def dil_proj(c):
                qi, qk, qr = QK.get()
                vi, vn, vr = VN.get()
                bi_, bb, br = BB.get()
                t_bb = sp.dma(bb[:], scratch[:, 2 * c:2 * c + 2, :], s_bb[c % 2], c // 2 + 1, br, mod_done, B["stored"])
                toks = {}
                for g in range(3):
                    for t_ in range(3):
                        n = 3 * g + t_
                        if c == 0 and n < 4:
                            i, b, t = first4[n]
                        else:
                            i, b, t = proj(8, ["dil_in"], HH, HL, h_ok)[0]
                        if t_ == 0:
                            u = fn(qk[:, 2 * g, :], b, ACT.Copy, t, qr, scale=0.125)
                            toks[(g, 0)] = u
                            bput(PB[0], i, u)
                        elif t_ == 1:
                            u = cp(dve, qk[:, 2 * g + 1, :], b, t, qr)
                            toks[(g, 1)] = u
                            bput(PB[0], i, u)
                        else:
                            if g == 2:
                                u = fn(VT[:, 2, :].rearrange("p (j a k) -> p j a k", j=4, a=4),
                                       b.rearrange("p (k a j) -> p j a k", k=32, a=4), ACT.Copy, t, vt_rel[0])
                            else:
                                u = fn(VT[:, g, :], b, ACT.Copy, t, vt_rel[0])
                            bput(PB[0], i, u)
                            i, b, rel = PB[0].get()
                            for j in range(4):
                                t = tpose(b[:, 128 * j:128 * j + 128], tok_view(VT[:, g, :], g % 2, j), C["ident"][:], rel, u,
                                          inc=(j == 3))
                            u = cp(dve, vn[:, 4 * g:4 * g + 4, :], b.rearrange("p (j f) -> p j f", j=4), t, vr)
                            toks[(g, 2)] = u
                            bput(PB[0], i, u)
                            vtl.append(t)
                            vt_rel[0] = []
                        if n % 3 == 2 and g == 2:
                            vt_rel[0] = list(vtl)
                            vtl.clear()
                        yield
                hs_pe[0] = [t]
                dl[c] = (qi, qk, vi, vn, bi_, bb, t_bb, toks)

            vtl = []

            def dil_att(c):
                qi, qk, vi, vn, bi_, bb, t_bb, toks = dl[c]
                NC = 24
                cm = small[:, 64:88].rearrange("p (j h) -> p j h", h=2)
                cn = small[:, 88:112].rearrange("p (j h) -> p j h", h=2)
                cs = small[:, 112:136].rearrange("p (j h) -> p j h", h=2)
                sds = []
                maxes = []
                g0off = [0, 128, 384, 640]
                g0wid = [128, 256, 256, 256]
                for hh in range(2):
                    half = 64 * hh
                    di, sd, dr = SD.get()
                    bk = [pool_b.get() for _ in range(4)]
                    hsl = slice(half, half + 64)
                    place = {}
                    for n in range(4):
                        b = bk[n // 2]
                        o = (0, 128)[n] if n < 2 else (0, 256)[n - 2]
                        w = g0wid[n]
                        ap = b[1][:, o:o + w]
                        t = mm(ap, qk[hsl, 0, n * 128:(n + 1) * 128], qk[hsl, 1, (n + 1) * 128 - w:(n + 1) * 128], True, True,
                               b[2], toks[(0, 0)], toks[(0, 1)], inc=True)
                        place[n] = (ap, bb[:, hh, 256 - w:256], sd[:, g0off[n]:g0off[n] + w], t)
                    for r in range(4):
                        b = bk[2]
                        ap = b[1][:, 128 * r:128 * r + 128]
                        t = mm(ap, tok_view(qk[hsl, 2, :], 1, r), tok_view(qk[hsl, 3, :], 1, r), True, True, b[2],
                               toks[(1, 0)], toks[(1, 1)], inc=True)
                        place[4 + r] = (ap, bb[:, hh, 256:384], sd[:, 896 + 128 * r:1024 + 128 * r], t)
                    b = bk[3]
                    for a_ in range(4):
                        for j in range(4):
                            r = 4 * a_ + j
                            t = mm(b[1][32 * j:32 * j + 32, 32 * a_:32 * a_ + 32], qk[hsl, 4, r:S:16], qk[hsl, 5, r:S:16],
                                   True, True, b[2], toks[(2, 0)], toks[(2, 1)], inc=(j == 3))
                        place[8 + a_] = (b[1][:, 32 * a_:32 * a_ + 32], bb[:, hh, 384:416],
                                         sd[:, 1408 + 32 * a_:1440 + 32 * a_], t)
                    for s_ in range(12):
                        ap, bias, dst, _ = place[s_]
                        t = place[(1, 3, 7, 11)[s_ // 2 if s_ < 4 else (2 if s_ < 8 else 3)]][3]
                        u = dve.do(lambda e, ap=ap, bias=bias, dst=dst, s_=s_, hh=hh: e.tensor_tensor_reduce(
                            out=dst, in0=ap, in1=bias, scale=1.0, scalar=-3.0e38, op0=ALU.add, op1=ALU.max,
                            accum_out=cm[:, s_, hh:hh + 1]), t, t_bb, dr, cmr[0])
                        q = s_ // 2 if s_ < 4 else (2 if s_ < 8 else 3)
                        bput(pool_b, bk[q][0], u)
                    maxes.append(u)
                    sds.append((di, sd, place))
                    yield
                BB.put(bi_, u)
                QK.put(qi, t)
                i, b, rel = pool_b.get()
                for s_ in range(12):
                    g, j = s_ // 4, s_ % 4
                    o = tok_view(b[32 * g:32 * g + 2, :], g, j)
                    rh = C["ident"][:] if g < 2 else C["ident"][:]
                    if g == 2:
                        o = b[64:66, :].rearrange("p (i a j) -> p a j i", i=32, a=4)[:, j, :, :]
                    t = mm(o, cm[:, s_, :], C["ident"][:], True, True, rel, maxes, inc=(s_ == 11))
                u = cp(dve, mrow[:], b[0:2, :], t, mrel[0], mod_done)
                u = tt(dve, mrow[:], mrow[:], b[32:34, :], ALU.max, u)
                u = tt(dve, mrow[:], mrow[:], b[64:66, :], ALU.max, u)
                cmr[0] = [t]
                bput(pool_b, i, u)
                yield
                i, b, rel = pool_b.get()
                for s_ in range(12):
                    g, j = s_ // 4, s_ % 4
                    o = b[:, 2 * s_:2 * s_ + 2]
                    if g < 2:
                        mm(o, tok_view(mrow[:], g, j), C["ident"][0:2, 0:2], True, True, rel, u)
                        continue
                    for z in range(4):
                        t = mm(o[32 * z:32 * z + 32, :], mrow[:, 4 * j + z:S:16], C["ident"][0:2, 0:2], True, True,
                               inc=(s_ == 11 and z == 3))
                mrel[0] = [t]
                un = ts(dve, cn, b[:, 0:24].rearrange("p (j h) -> p j h", h=2), -1.0, None, ALU.mult, None, t, cnr[0])
                bput(pool_b, i, un)
                yield
                exps = []
                for hh in range(2):
                    di, sd, place = sds[hh]
                    for s_ in range(12):
                        dst = place[s_][2]
                        v = fn(dst, dst, ACT.Exp, un, maxes[hh], csr[0], bias=cn[:, s_, hh:hh + 1], acc=cs[:, s_, hh:hh + 1])
                    exps.append(v)
                cnr[0] = [v]
                yield
                i, b, rel = pool_b.get()
                for s_ in range(12):
                    g, j = s_ // 4, s_ % 4
                    o = tok_view(b[0:2, :], g, j)
                    if g == 2:
                        o = b[0:2, :].rearrange("p (i a j) -> p a j i", i=32, a=4)[:, j, :, :]
                    t = mm(o, cs[:, s_, :], C["ident"][:], s_ == 0, s_ == 11, rel, exps, inc=(s_ == 11), skip=True)
                csr[0] = [t]
                u = recip(mrow[:], b[0:2, :], t, mrel[0])
                bput(pool_b, i, u)
                oi, o_, orel = OBD.get()
                for hh in range(2):
                    di, sd, place = sds[hh]
                    half = 64 * hh
                    cpt = {}
                    srcs = [sd[:, 128 * z:128 * z + 128] for z in range(12)]
                    for z3 in range(3):
                        i, b, rel = pool_b.get()
                        for z in range(4):
                            t = tpose(b[:, 128 * z:128 * z + 128], srcs[4 * z3 + z], C["ident"][:], rel, exps[hh],
                                      inc=(z == 3))
                        if z3 < 2:
                            cpt[z3] = fn(PD[:, 512 * z3:512 * z3 + 512], b, ACT.Copy, t, pdr[0])
                            bput(pool_b, i, cpt[z3])
                        else:
                            v1 = fn(PD[:, 1024:1408], b[:, 0:384], ACT.Copy, t, pdr[0])
                            vv = []
                            for a_ in range(4):
                                vv.append(ts(dve, RB[:, :, a_, :], b[:, 384:512].rearrange("p (j i) -> p j i", j=4),
                                             C["adiag"][:, a_:a_ + 1], None, ALU.mult, None, t, v1, pdr[0], mod_done))
                            cpt[2] = [v1] + vv
                            bput(pool_b, i, v1, vv)
                    SD.put(di, t)
                    blk = 0
                    oh_ = o_[half:half + 64, :]
                    fs = slice(64 * hh, 64 * hh + 64)
                    for n in range(4):
                        for c_ in ((1,) if n == 0 else (0, 1)):
                            t = mm(oh_[:, n * 128:(n + 1) * 128], vn[:, n - 1 + c_, fs], PD[:, 128 * blk:128 * blk + 128],
                                   blk == 0, False, orel, cpt[blk // 4], toks[(0, 2)], skip=True)
                            blk += 1
                    for r in range(4):
                        mm(tok_view(oh_, 1, r), vn[:, 4 + r, fs], PD[:, 128 * blk:128 * blk + 128], False, False,
                           cpt[blk // 4], toks[(1, 2)], skip=True)
                        blk += 1
                    for j in range(4):
                        o = oh_.rearrange("p (i a j) -> p j a i", i=32, a=4)[:, j, :, :]
                        t = mm(o, vn[:, 8 + j, fs], RB[:, j, :, :], False, j == 3, cpt[2], toks[(2, 2)], inc=(j == 3), skip=True)
                    pdr[0] = [t]
                    yield
                VN.put(vi, t)
                i, b, rel = pool_b.get()
                t2 = mm(b, C["sel"][0:2, :], mrow[:], True, True, rel, u, t_const["sel"], inc=True)
                mrel[0] = [t2]
                i0, z, r0 = T.get()
                u = fn(z, b, ACT.Copy, t2, r0)
                bput(pool_b, i, u)
                u = tt(dve, YF[:, c, :], z, o_, ALU.mult, u, t)
                bput(OBD, oi, u)
                T.put(i0, u)
                yf_tok[c] = u
                yield

            cmr, cnr, csr, mrel, pdr, yf_tok = [[]], [[]], [[]], [[]], [[]], {}
            gp = dil_proj(0)
            for _ in range(4):
                next(gp)
            PBX = banks(4, 5, 6)
            PB[0] = PBX
            OBD = banks(7)
            for _ in gp:
                pass
            for c in range(8):
                if c < 7:
                    weave(dil_proj(c + 1), dil_att(c), 1)
                else:
                    for _ in dil_att(c):
                        pass
            PB[0] = banks(0, 1, 2, 3, 4, 5, 6, 7)
            y_ok = {m: split_out(HH[:, m, :], HL[:, m, :], YF[:, m, :], [yf_tok[m], hs_pe[0]]) for m in range(8)}
            phase_tok[:] = [y_ok[m] for m in range(8)]
            guard()
            Y = at("Ydil", ph + 45056, [P, 8, S])
            out_proj("dil_o", y_ok, lambda m, pb: y_store(Y, m, pb, 2, None), None, lambda k: (HH, HL, k))
            post_norm(Y, 1, 1)
            second_ffn(1, 1)
            assert W["tile"] == len(tiles)
            return sp.dma(out, X[:], s_c[7], 1, x_tok)
        t_out = body()

        block = ctx.enter_context(nc.Block())

        def play(q, eng, extra=()):
            pend_ = []
            for need, f, inc in q.ops:
                for s_, v in need:
                    eng.wait_ge(s_, v)
                if f is None:
                    continue
                ins = f(eng)
                if inc:
                    ins.then_inc(q.sem, 1)
            for w in extra:
                eng.wait_ge(w[1], w[2])

        @block.sync
        def _(e):
            play(sp, e, [B["stored"], t_out])

        @block.scalar
        def _(e):
            play(act, e)

        @block.vector
        def _(e):
            play(dve, e)

        @block.gpsimd
        def _(e):
            play(pool, e)

        @block.tensor
        def _(e):
            play(pe, e)


def matrices(a):
    m = {}
    ev = a["ev_w_in"][0]
    m["ev_in"] = ev
    m["ev_out"] = a["ev_w_out"][0]
    od = a["od_w_in"][0]
    order = [h for t in range(2) for j in range(4) for h in (8 * t + j, 8 * t + 4 + j)]
    q = od[:, :1024].reshape(1024, 16, 64)[:, order].reshape(1024, 1024)
    m["od_in"] = np.concatenate([q, od[:, 1024:]], axis=1)
    m["od_out"] = a["od_w_out"][0].reshape(16, 64, 1024)[order].reshape(1024, 1024)
    for l in range(2):
        m["f%dg" % l] = a["ffn_w_gate"][l]
        m["f%du" % l] = a["ffn_w_up"][l]
        for half in range(2):
            m["f%dd%d" % (l, half)] = a["ffn_w_down"][l][1408 * half:1408 * half + 1408]
    for l in range(2):
        for w in range(2):
            t = "ab"[l] + str(w)
            m[t + "g"] = a["ffn_w_gate_2"][l, w]
            m[t + "u"] = a["ffn_w_up_2"][l, w]
            for half in range(2):
                m[t + "d%d" % half] = a["ffn_w_down_2"][l, w][1408 * half:1408 * half + 1408]
    wi = a["mla_w_in_2"][0]
    kr = wi[:, 640:672]
    sw = np.concatenate([kr[:, 16:], kr[:, :16]], axis=1)
    m["mla_in"] = np.concatenate([wi[:, :640], kr, kr, kr, sw], axis=1)
    qu = a["mla_w_q_up_2"][0].reshape(384, 16, 96)
    m["mla_q"] = np.concatenate([qu, qu[:, :, 80:96], qu[:, :, 64:80]], axis=2).reshape(384, 2048)
    kv = a["mla_w_kv_up_2"][0].reshape(256, 16, 128)
    m["mla_k"] = kv[:, :, :64].reshape(256, 1024)
    m["mla_v"] = kv[:, :, 64:].reshape(256, 1024)
    m["mla_o"] = a["mla_w_o_2"][0]
    m["dil_in"] = a["dil_w_in_2"][0]
    m["dil_o"] = a["dil_w_o_2"][0]
    return m


def pack_stream(a):
    m = matrices(a)
    tiles = tile_list()
    nb = (len(tiles) + BT - 1) // BT
    out = np.zeros((nb, P, BT * 128), np.float32)
    for t, (name, k, c) in enumerate(tiles):
        b, o = divmod(t, BT)
        out[b, :, o * 128:(o + 1) * 128] = m[name][k * 128:(k + 1) * 128, c * 128:(c + 1) * 128]
    return out


def pack_mod(a):
    out = np.empty((240, P, 1024), np.float32)
    n = 0
    for w, nv in ((a["ada_w"], 6), (a["w_mod_2"], 9)):
        for l in range(2):
            for v in range(nv):
                for k in range(8):
                    out[n] = w[l][k * 128:(k + 1) * 128, v * 1024:(v + 1) * 1024]
                    n += 1
    return out


def pack_vec(a):
    cols, n = columns()
    out = np.zeros((P, n), np.float32)

    def put(name, v):
        s, w = cols[name]
        out[:, s:s + w] = np.ascontiguousarray(v).reshape(w, P).T

    put("c", a["c"])
    put("c2", a["c_2"])
    put("ada_b", a["ada_b"])
    put("mix_g", a["norm_mix_g"])
    put("ffn_g", a["norm_ffn_g"])
    put("cw", a["ev_conv_w"])
    put("cb", a["ev_conv_b"])
    put("ba", a["ev_ba"])
    put("bx", a["ev_bx"])
    put("lam", a["ev_lam"])
    for n_, k in (("evq", "ev_qn_g"), ("evk", "ev_kn_g"), ("odq", "od_qn_g"), ("odk", "od_kn_g")):
        put(n_, np.concatenate([a[k][0], a[k][0]]))
    put("fcw", a["ffn_conv_w"])
    put("fcb", a["ffn_conv_b"])
    put("pre", a["norm_pre_2"])
    put("post", a["norm_post_2"])
    put("b_mod", a["b_mod_2"])
    put("mq", a["mla_q_norm_2"])
    put("mkv", a["mla_kv_norm_2"])
    s, w = cols["sinks"]
    out[:, s:s + w] = a["od_sinks"][0][None, :]
    return out


def kernel(**inputs):
    import concourse.bacc as bacc
    from concourse.bass_utils import run_bass_kernel_spmd as run

    a = {k: np.asarray(v) for k, v in inputs.items()}
    consts = const_arrays()
    wax = np.zeros((P, 8, P), np.float32)
    for g, k in enumerate(("ev_wa", "ev_wx")):
        for n in range(8):
            o = 64 * (n % 2)
            wax[o:o + 64, 4 * g + n // 2, o:o + 64] = a[k][0, n]
    arrays = {
        "xt": np.ascontiguousarray(a["x"][0].T.reshape(8, P, S).transpose(1, 0, 2)),
        "wst": pack_stream(a),
        "mst": pack_mod(a),
        "vec": pack_vec(a),
        "cst": np.concatenate([consts[n] for n, _ in CONST_WIDTHS], axis=1),
        "trig": consts["trig"],
        "oh": onehots(),
        "tab": np.ascontiguousarray(a["rel_bias_2"]),
        "wax": wax,
    }
    nc = bacc.Bacc("TRN2", target_bir_lowering=False, num_devices=1)
    aps = {n: nc.dram_tensor(n, v.shape, F32, kind="ExternalInput").ap() for n, v in arrays.items()}
    o = nc.dram_tensor("out", (P, 8, S), F32, kind="ExternalOutput").ap()
    sc = nc.dram_tensor("scratch", (P, 16, 416), F32, kind="Internal").ap()
    program(nc, out=o, scratch=sc, **aps)
    r = run(nc, [arrays], core_ids=[0])
    got = np.asarray(r.results[0]["out"])
    return np.ascontiguousarray(got.transpose(1, 0, 2).reshape(1024, S).T)[None]
```

```python
import math
from contextlib import ExitStack

import numpy as np

import concourse.bass as bass
from concourse import mybir

F32 = mybir.dt.float32
F32R = mybir.dt.float32r
ACT = mybir.ActivationFunctionType
ALU = mybir.AluOpType
AX = mybir.AxisListType

EPS = 1e-6
NEG = -float(2.0 ** 100)
S = 512
P = 128
BT = 8
RAW, SPLIT = 5, 3
MLA_SCALE = 96.0 ** -0.5


def even_groups():
    gs = [(8, [("ev_in", 0), ("ev_in", 4), ("ev_in", 1), ("ev_in", 5)]),
          (8, [("ev_in", 2), ("ev_in", 6), ("ev_in", 3), ("ev_in", 7)]),
          (8, [("ev_in", 16 + i) for i in range(4)])]
    gs += [(8, [("ev_in", 8 + i)]) for i in range(8)]
    return gs + [(8, [("ev_out", i)]) for i in range(8)]


def odd_groups():
    gs = [(8, [("od_in", i) for i in range(4)])]
    gs += [(8, [("od_in", i)]) for i in range(4, 10)]
    gs += [(8, [("od_in", 10), ("od_in", 11)])]
    return gs + [(8, [("od_out", i)]) for i in range(8)]


def ffn_groups(tag):
    gs = []
    for half in (0, 1):
        at = 11 * half
        if half == 0:
            gs.append((8, [(tag + "g", 0), (tag + "u", 0), (tag + "g", 1), (tag + "u", 1)]))
            at = 2
        for i in range(at, 11 * half + 11):
            gs.append((8, [(tag + "g", i), (tag + "u", i)]))
        gs += [(11, [(tag + "d%d" % half, i)]) for i in range(8)]
    return gs


def mla_groups():
    gs = [(8, [("mla_in", i) for i in range(6)])]
    gs += [(2, [("mla_v", 4 * f + i) for i in range(4)]) for f in range(2)]
    for h in range(16):
        gs.append((3, [("mla_q", h)]))
        if h % 2 == 0:
            gs.append((2, [("mla_k", h // 2)]))
    return gs + [(8, [("mla_o", i)]) for i in range(8)]


def dil_groups():
    gs = []
    for c in range(8):
        tiles = [("dil_in", 72 * 0 + 24 * g + 8 * t + c) for g in range(3) for t in range(3)]
        if c == 0:
            gs.append((8, tiles[:4]))
            tiles = tiles[4:]
        gs += [(8, [t]) for t in tiles]
    return gs + [(8, [("dil_o", i)]) for i in range(8)]


def plan():
    gs = even_groups() + ffn_groups("f0") + odd_groups() + ffn_groups("f1")
    gs += ffn_groups("a0") + mla_groups() + ffn_groups("a1")
    gs += ffn_groups("b0") + dil_groups() + ffn_groups("b1")
    return gs


def tile_list():
    return [(name, k, m) for nk, cols in plan() for k in range(nk) for name, m in cols]


def columns():
    at, out = 0, {}
    for name, width in [
        ("c", 8), ("c2", 8), ("ada_b", 96), ("mix_g", 16), ("ffn_g", 16), ("cw", 16), ("cb", 4),
        ("ba", 4), ("bx", 4), ("lam", 4), ("evq", 1), ("evk", 1), ("odq", 1), ("odk", 1),
        ("fcw", 132), ("fcb", 44), ("pre", 48), ("post", 48), ("b_mod", 144), ("mq", 3), ("mkv", 2),
        ("sinks", 16),
    ]:
        out[name] = (at, width)
        at += width
    return out, at


def const_arrays():
    i = np.arange(P)
    c = {}
    c["ident"] = np.eye(P)
    c["ones"] = np.ones((P, P))
    c["blk"] = (i[:, None] // 64 == i[None, :] // 64) * 1.0
    c["later"] = (i[:, None] > i[None, :]) * 1.0
    c["tri"] = (i[:, None] < i[None, :]) * 1.0
    c["caus"] = np.where(i[None, :] <= i[:, None], 0.0, NEG)
    j = np.arange(256)
    c["band"] = np.where((j[None, :] > i[:, None]) & (j[None, :] <= i[:, None] + 128), 0.0, NEG)
    c["adiag"] = (i[:, None] // 32 == np.arange(4)[None, :]) * 1.0
    sel = np.zeros((P, P))
    sel[0, :64] = 1.0
    sel[1, 64:] = 1.0
    c["sel"] = sel
    half = 16
    freqs = np.float32(10000.0) ** (-np.arange(half, dtype=np.float32) / np.float32(half))
    ang = (np.arange(S, dtype=np.float32)[:, None] * freqs[None, :].astype(np.float32)).astype(np.float64)
    cos, sin = np.cos(ang).T, np.sin(ang).T
    trig = np.zeros((P, S))
    trig[64:80], trig[80:96] = cos, cos
    trig[96:112], trig[112:128] = -sin, sin
    c["trig"] = trig
    return {k: v.astype(np.float32) for k, v in c.items()}


CONST_WIDTHS = [("ident", 128), ("ones", 128), ("blk", 128), ("later", 128), ("tri", 128), ("caus", 128),
                ("band", 256), ("adiag", 4), ("sel", 128)]


def bucket(dist):
    d = np.maximum(dist, 1).astype(np.float32)
    large = 16 + (np.log(d / np.float32(16)) / np.float32(math.log(2048 / 16)) * np.float32(16)).astype(np.int32)
    return np.where(dist < 16, dist, np.minimum(large, 31))


def onehots():
    def table(rel, dil):
        ok = (rel >= 0) & (rel <= 128)
        b = np.where(ok, bucket(np.maximum(rel, 0) * dil), 32)
        return (np.arange(33)[:, None] == b[None, :]).astype(np.float32)

    o0 = table(np.arange(384) - 127, 1)
    o1 = table(np.arange(256) - 127, 4)
    o2 = table(np.arange(64) - 31, 16)
    return np.ascontiguousarray(np.concatenate([o0, o1, o2], axis=1)[:, ::-1])


class Queue:

    def __init__(self, sem):
        self.sem, self.n, self.ops, self.seen = sem, 0, [], {}

    def do(self, fn, *waits, inc=True):
        need = []
        for w in flat(waits):
            key, sem, value = w
            if self.seen.get(key, 0) < value:
                self.seen[key] = value
                need.append((sem, value))
        self.ops.append((need, fn, 1 if inc else 0))
        if inc:
            self.n += 1
            return (id(self), self.sem, self.n)
        return None

    def dma(self, out, in_, sem, count, *waits):
        need = []
        for w in flat(waits):
            key, s, value = w
            if self.seen.get(key, 0) < value:
                self.seen[key] = value
                need.append((s, value))
        self.ops.append((need, lambda e: e.dma_start(out, in_).then_inc(sem, 16), 0))
        return (id(sem), sem, 16 * count)

    def play(self, eng):
        for need, fn, inc in self.ops:
            for sem, value in need:
                eng.wait_ge(sem, value)
            ins = fn(eng)
            if inc:
                ins.then_inc(self.sem, 1)


def flat(x):
    if x is None:
        return []
    if isinstance(x, tuple) and len(x) == 3 and isinstance(x[2], int):
        return [x]
    return [y for z in x for y in flat(z)]


class Ring:

    def __init__(self, bufs):
        self.bufs, self.rel, self.at = bufs, [[] for _ in bufs], 0

    def get(self):
        i = self.at
        self.at = (i + 1) % len(self.bufs)
        rel, self.rel[i] = self.rel[i], None
        assert rel is not None, "a buffer is taken before it is given back"
        return i, self.bufs[i], rel

    def put(self, i, *tokens):
        self.rel[i] = list(tokens)

    def all(self):
        return list(self.rel)


def weave(main, side, every=1):
    n, live = 0, True
    for _ in main:
        n += 1
        if live and n % every == 0:
            live = next(side, "end") != "end"
    for _ in side:
        pass


def program(nc, xt, wst, mst, vec, cst, trig, oh, tab, flip, wax, out, bvec, scratch):
    with ExitStack() as ctx:
        sem = lambda n: ctx.enter_context(nc.semaphore(n))
        base = 16512
        limit = 229368
        pos = [base]
        ctx.enter_context(nc.sbuf_tensor("arena", [P, (limit - base) // 4 - 16], F32))

        def at(name, offset, shape, dt=F32):
            n = 4
            for s in shape[1:]:
                n *= s
            assert offset + n <= limit, (name, offset + n, limit)
            return nc.alloc_sbuf_tensor_at(name, shape, dt, offset=offset)

        def sb(name, shape, dt=F32):
            n = 4
            for s in shape[1:]:
                n *= s
            t = at(name, pos[0], shape, dt)
            pos[0] += (n + 31) // 32 * 32
            return t

        cols, ncols = columns()
        pe, dve, act, pool, sp = (Queue(sem("s_" + n)) for n in ("pe", "dve", "act", "pool", "sp"))

        X = sb("X", [P, 8, S])
        hh_off = pos[0]
        HH = sb("HH", [P, 8, S], F32R)
        hl_off = pos[0]
        HL = sb("HL", [P, 8, S], F32R)
        wraw = sb("wraw", [P, RAW, BT * 128])
        whi = sb("whi", [P, SPLIT, BT * 128], F32R)
        wlo = sb("wlo", [P, SPLIT, BT * 128], F32R)
        mraw = sb("mraw", [P, 2, 1024])
        macc_off = pos[0]
        macc = sb("macc", [P, 1024])
        V = sb("V", [P, ncols])
        C = {}
        for n, w in CONST_WIDTHS:
            C[n] = sb("c_" + n, [P, w])
        identr = sb("identr", [P, P], F32R)
        causr = sb("causr", [P, P], F32R)
        bandr = sb("bandr", [P, 256], F32R)
        SILU = sb("SILU", [P, 16])
        MOD = sb("MOD", [P, 30, 8])
        AM = sb("AM", [P, 10, 8])
        GM = sb("GM", [P, 6, 8])
        CF = sb("CF", [P, 4])
        QS = sb("QS", [P, 2])
        EPSC = sb("EPSC", [P, 1])
        SQ = sb("SQ", [P, S])
        RS = sb("RS", [P, 2, S])
        TT = sb("TT", [P, 4, S])
        small = sb("small", [P, 160])
        ph = pos[0]
        ps = ctx.enter_context(nc.psum_tensor("ps", [P, 8, 512], F32))

        TX = at("TX", ph + 77824, [P, S])
        T = Ring([TT[:, i, :] for i in range(4)] + [TX[:]])
        RSR = Ring([RS[:, i, :] for i in range(2)])
        PB = [None]

        def banks(*idx):
            r = Ring([ps[:, i, :] for i in idx])
            r.idx = idx
            r.rel = [bankrel[i] for i in idx]
            for j, i in enumerate(idx):
                r.rel[j] = list(bankrel[i])
            return r

        bankrel = [[] for _ in range(8)]

        def bput(r, i, *tokens):
            r.put(i, *tokens)
            bankrel[r.idx[i]] = list(tokens)

        def col(name, i=0, w=1):
            a = cols[name][0] + i
            return V[:, a:a + w]

        def mm(o, l, r, start, stop, *waits, inc=False, skip=False):
            return pe.do(lambda e: e.matmul(o, l, r, start=start, stop=stop, skip_group_check=skip), *waits, inc=inc)

        def tpose(o, i, ident, *waits, inc=False):
            return pe.do(lambda e: e.transpose(o, i, ident), *waits, inc=inc)

        def fn(o, i, f, *waits, scale=1.0, bias=0.0, acc=None):
            if acc is None:
                return act.do(lambda e: e.activation(o, i, f, bias=bias, scale=scale), *waits)
            return act.do(lambda e: e.activation(o, i, f, bias=bias, scale=scale, accum_out=acc), *waits)

        def tt(q, o, a, b, op, *waits):
            return q.do(lambda e: e.tensor_tensor(o, a, b, op), *waits)

        def ts(q, o, a, s1, s2, op0, op1, *waits):
            if s2 is None:
                return q.do(lambda e: e.tensor_scalar(o, a, s1, None, op0), *waits)
            return q.do(lambda e: e.tensor_scalar(o, a, s1, s2, op0, op1), *waits)

        def stt(o, a, s, b, op0, op1, *waits):
            return dve.do(lambda e: e.scalar_tensor_tensor(o, a, s, b, op0, op1), *waits)

        def recip(o, i, *waits):
            return dve.do(lambda e: e.reciprocal(o, i), *waits)

        def scan(o, a, b, *waits):
            return dve.do(lambda e: e.tensor_tensor_scan(o, a, b, 0.0, ALU.mult, ALU.add), *waits)

        def cp(q, o, i, *waits):
            return q.do(lambda e: e.tensor_copy(o, i), *waits)

        s_c = [sem("s_c%d" % i) for i in range(8)]
        t_vec = sp.dma(V[:], vec, s_c[0], 1)
        t_const = {}

        tiles = tile_list()
        nblocks = (len(tiles) + BT - 1) // BT
        s_w = [sem("s_w%d" % i) for i in range(RAW)]
        W = {"tile": 0, "dma": 0, "split": 0, "eng": dve}
        w_load, w_hi, w_lo, w_pe = {}, {}, {}, {}

        def w_dma():
            b = W["dma"]
            if b >= nblocks:
                return
            rel = [w_hi[b - RAW], w_lo[b - RAW]] if b >= RAW else []
            w_load[b] = sp.dma(wraw[:, b % RAW, :], wst[b], s_w[b % RAW], b // RAW + 1, rel)
            W["dma"] += 1

        def w_split():
            b = W["split"]
            if b >= nblocks:
                return
            rel = [w_pe[b - SPLIT]] if b >= SPLIT else []
            r, h, l = wraw[:, b % RAW, :], whi[:, b % SPLIT, :], wlo[:, b % SPLIT, :]
            w_hi[b] = fn(h, r, ACT.Copy, w_load[b], rel)
            w_lo[b] = tt(W["eng"], l, r, h.bitcast(F32), ALU.subtract, w_hi[b], rel)
            W["split"] += 1

        s_m = [sem("s_m%d" % i) for i in range(2)]
        M = {"n": 0, "acc": [], "pe": {0: [], 1: []}, "sum": None, "hold": 0}
        m_tok = {}
        m_use, m_ld = {}, {}
        MR0 = at("MR0", ph, [P, 16, 1024])
        MACC2 = at("MACC2", ph + 65536, [P, 1024])
        s_m0 = [sem("s_m0_%d" % i) for i in range(16)]

        def mod_dma(n):
            if n < 16:
                m_ld[n] = sp.dma(MR0[:, n, :], mst[n], s_m0[n], 1)
            elif n < 240:
                m_ld[n] = sp.dma(mraw[:, n % 2, :], mst[n], s_m[n % 2], (n - 16) // 2 + 1, m_use[n - 2] if n >= 18 else [])

        def mod_step():
            n = M["n"]
            if n >= 240:
                return
            v, k = n // 8, n % 8
            if n >= 15:
                if n + 1 not in m_ld:
                    mod_dma(n + 1)
            ld = m_ld[n]
            raw = MR0[:, n, :] if n < 16 else mraw[:, n % 2, :]
            cc = SILU[:, k:k + 1] if v < 12 else SILU[:, 8 + k:9 + k]
            acc = MACC2 if v == 1 else macc
            if k == 0:
                t = ts(dve, acc[:], raw, cc, None, ALU.mult, None, ld, t_silu, M["pe"][v == 1])
            else:
                t = stt(acc[:], raw, cc, acc[:], ALU.mult, ALU.add, ld, M["acc"])
            m_use[n] = t
            M["acc"] = t
            M["n"] += 1
            if k == 7:
                M["sum"] = (v, t)

        def mod_sum():
            if M["sum"] is None:
                return False
            v, t = M["sum"]
            acc = MACC2 if v == 1 else macc
            i, b, rel = PB[0].get()
            for j in range(8):
                last = mm(b[:, j:j + 1], acc[:, j * 128:(j + 1) * 128], C["ones"][:, 0:1], True, True,
                          rel, t, t_const["ones"], inc=(j == 7))
            bias = col("ada_b", 8 * v, 8) if v < 12 else col("b_mod", 8 * (v - 12), 8)
            m_tok[v] = tt(dve, MOD[:, v, :], b[:, 0:8], bias, ALU.add, last)
            M["pe"][v == 1] = last
            M["sum"] = None
            bput(PB[0], i, m_tok[v])
            return True

        def mod_ready(v):
            while v not in m_tok:
                if not mod_sum():
                    mod_step()
            return m_tok[v]

        def w_block_start(b):
            while W["dma"] < min(b + RAW, nblocks):
                w_dma()
                if b > 0:
                    break
            while W["split"] < min(b + SPLIT, nblocks):
                w_split()
            if M["hold"]:
                M["hold"] -= 1
            elif b > 0 and not mod_sum():
                mod_step()

        def next_tiles(n, expect):
            t = W["tile"]
            b, o = t // BT, t % BT
            assert o + n <= BT
            assert [x[0] for x in tiles[t:t + n]] == expect, (tiles[t:t + n], expect)
            if o == 0:
                w_block_start(b)
            W["tile"] += n
            last = (o + n == BT) or W["tile"] == len(tiles)
            sl = slice(o * 128, (o + n) * 128)
            return b, whi[:, b % SPLIT, sl], wlo[:, b % SPLIT, sl], [w_hi[b], w_lo[b]], last

        def proj(nk, names, srch, srcl, ready, k0=0):
            got = [PB[0].get() for _ in names]
            ends = [None] * len(names)
            for k in range(nk):
                for m, name in enumerate(names):
                    b, wh, wl, w_ok, last = next_tiles(1, [name])
                    o = got[m][1]
                    waits = [w_ok, ready[k0 + k]] + ([got[m][2]] if k == 0 else [])
                    mm(o, wh, srch[:, k0 + k, :], k == 0, False, waits)
                    mm(o, wh, srcl[:, k0 + k, :], False, False)
                    fin = k == nk - 1
                    t = mm(o, wl, srch[:, k0 + k, :], False, fin, inc=last or fin)
                    if last:
                        w_pe[b] = t
                    if fin:
                        ends[m] = t
            return [(got[m][0], got[m][1], ends[m]) for m in range(len(names))]

        def proj_rows(nk, names, srch, srcl, ready):
            n = len(names)
            got = [PB[0].get() for _ in range(4)]
            ends = [None] * 4
            for k in range(nk):
                b, wh, wl, w_ok, last = next_tiles(n, names)
                for q in range(4):
                    o = got[q][1][:, 0:128 * n]
                    hs, ls = srch[:, k, q * 128:(q + 1) * 128], srcl[:, k, q * 128:(q + 1) * 128]
                    waits = [w_ok, ready[k]] + ([got[q][2]] if k == 0 else [])
                    mm(o, hs, wh, k == 0, False, waits)
                    mm(o, ls, wh, False, False)
                    fin = k == nk - 1
                    t = mm(o, hs, wl, False, fin, inc=(last and q == 3) or fin)
                    if fin:
                        ends[q] = t
                if last:
                    w_pe[b] = t
            return [(got[q][0], got[q][1], ends[q]) for q in range(4)]

        def set_table(name):
            act.do(lambda e: e.preload_act_table_set(name), inc=False)

        for n in range(2):
            mod_dma(n)
        t_cst = []
        a = 0
        s_cc = [sem("s_cc%d" % i) for i in range(len(CONST_WIDTHS))]
        for q, (n, w) in enumerate(CONST_WIDTHS):
            t_cst.append(sp.dma(C[n][:], cst[:, a:a + w], s_cc[q], 1))
            a += w
        t_const.update({n: t_cst[q] for q, (n, w) in enumerate(CONST_WIDTHS)})

        t_x = sp.dma(X[:], xt, s_c[1], 1)
        for n in range(2, 16):
            mod_dma(n)
        for b in range(RAW):
            w_dma()

        t_idr = cp(dve, identr[:], C["ident"][:], t_const["ident"])
        t_car = cp(dve, causr[:], C["caus"][:], t_const["caus"])
        t_bar = cp(dve, bandr[:], C["band"][:], t_const["band"])
        t_eps = pool.do(lambda e: e.memset(EPSC[:], EPS))
        t_silu = fn(SILU[:], V[:, 0:16], ACT.Silu, t_vec)
        act.seen[t_vec[0]] = t_vec[2]
        lamc = col("lam", 0, 4)
        sm = small
        u = fn(sm[:, 0:4], lamc, ACT.Abs, t_vec)
        u = fn(sm[:, 0:4], sm[:, 0:4], ACT.Exp, u, scale=-1.0)
        u = fn(sm[:, 0:4], sm[:, 0:4], ACT.Ln, u, bias=1.0)
        t = ts(dve, sm[:, 4:8], lamc, -1.0, 0.0, ALU.mult, ALU.max, t_vec)
        t = tt(dve, sm[:, 4:8], sm[:, 4:8], sm[:, 0:4], ALU.add, t, u)
        t_cf = ts(dve, CF[:], sm[:, 4:8], -8.0, None, ALU.mult, None, t)
        t_qs = ts(dve, QS[:, 0:1], col("evq"), 0.125, None, ALU.mult, None, t_vec)
        t_qs = ts(dve, QS[:, 1:2], col("odq"), 0.125, None, ALU.mult, None, t_vec)

        PB[0] = banks(4, 5, 6, 7)
        B = {}

        x_tok = [t_x] * 8
        hs_pe = []

        def sq_add(m, src, tok, st):
            if m == 0:
                st["sq"] = fn(SQ[:], src, ACT.Square, tok, st["free"])
                return
            i, b, rel = T.get()
            u = fn(b, src, ACT.Square, tok, rel)
            if m == 7:
                st["last"] = (i, b, u)
                return
            st["sq"] = tt(dve, SQ[:], SQ[:], b, ALU.add, u, st["sq"])
            T.put(i, st["sq"])

        SQS = {"free": [], "sq": None}

        def sum_open():
            i, b, rel = PB[0].get()
            return {"i": i, "b": b, "rel": rel, "n": 0}

        def sum_add(S_, buf, tok, last):
            t = mm(S_["b"], C["ones"][:], buf, S_["n"] == 0, last, S_["rel"], tok, t_const["ones"], inc=True)
            S_["n"] += 1
            return t

        def rsqrt_of(sb_, n, w, q, done):
            k, y, rr = RSR.get()
            i1, m_, r1 = T.get()
            u = fn(y, sb_, ACT.Ln, w, rr, t_eps, bias=EPSC[:, 0:1], scale=1.0 / n)
            v = ts(dve, m_, sb_, -0.5 / n, -0.5 * EPS, ALU.mult, ALU.add, u, r1)
            done(u, v)
            u = fn(y, y, ACT.Exp, u, scale=-0.5)
            u = fn(q, y, ACT.Square, u, w)
            yield
            t = tt(dve, q, q, m_, ALU.mult, u, v)
            T.put(i1, t)
            t = stt(y, q, 1.5, y, ALU.add, ALU.mult, t)
            yield k, y, t

        def sum_close(S_, n, t):
            i0, q, r0 = T.get()
            z = rsqrt_of(S_["b"], n, [t, r0], q, lambda *a: bput(PB[0], S_["i"], *a))
            next(z)
            k, y, t = next(z)
            T.put(i0, t)
            return k, y, t

        def total_open(st):
            S_ = sum_open()
            t = sum_add(S_, SQ[:], st["sq"], False)
            st["free"] = t
            i, b, u = st["last"]
            t = sum_add(S_, b, u, True)
            T.put(i, t)
            return S_, t

        def total(st, n):
            S_, t = total_open(st)
            return sum_close(S_, n, t)

        def modulate(shift, amul, t_mod, got=None):
            j, R, tr = got or total(SQS, 1024)
            toks = []

            def low(m, i, b, u):
                v = stt(HL[:, m, :], b, shift[:, m:m + 1], HH[:, m, :].bitcast(F32), ALU.add, ALU.subtract, u, hs_pe[0])
                T.put(i, v)
                toks.append([u, v])

            prev = None
            for m in range(8):
                i, b, rel = T.get()
                t = stt(b, X[:, m, :], amul[:, m:m + 1], R, ALU.mult, ALU.mult, tr, x_tok[m], t_mod, rel)
                u = fn(HH[:, m, :], b, ACT.Identity, t, t_mod, hs_pe[0], bias=shift[:, m:m + 1])
                if prev:
                    low(*prev)
                prev = (m, i, b, u)
            low(*prev)
            RSR.put(j, t)
            return toks

        hs_pe.append([])

        def amul(idx, v, gain):
            t = mod_ready(v)
            return stt(AM[:, idx, :], MOD[:, v, :], 1.0, gain, ALU.add, ALU.mult, t, t_vec)

        def residual(m, pb, gate, t_gate, last_q):
            i, b, t = pb
            u = stt(X[:, m, :], b, gate[:, m:m + 1], X[:, m, :], ALU.mult, ALU.add, t, t_gate, x_tok[m])
            bput(PB[0], i, u)
            x_tok[m] = u
            return u

        def split_out(dh, dl, src, waits):
            u = fn(dh, src, ACT.Copy, waits)
            v = tt(dve, dl, src, dh.bitcast(F32), ALU.subtract, u)
            return [u, v]

        def ffn(tag, ready, conv, sink):
            PH = at("PH" + tag, ph, [P, 11, S], F32R)
            PL = at("PL" + tag, ph + 22528, [P, 11, S], F32R)
            PB[0] = banks(0, 1, 2, 3, 4, 5, 6, 7)
            down = [[], []]
            set_table("silu_and_others")

            def product(i, half, g, u):
                gi, gb, gt = g
                ui, ub, ut = u
                k = i - 11 * half
                i0, a_, r0 = T.get()
                if conv is not None:
                    cw, cb = cols["fcw"][0] + 66 * conv, cols["fcb"][0] + 22 * conv
                    w = lambda j: V[:, cw + 22 * j + i:cw + 22 * j + i + 1]
                    i1, y, r1 = T.get()
                    t = fn(y, gb, ACT.Identity, gt, r1, bias=V[:, cb + i:cb + i + 1], scale=w(2))
                    t = stt(y[:, 1:S], gb[:, 0:S - 1], w(1), y[:, 1:S], ALU.mult, ALU.add, t)
                    t = stt(y[:, 2:S], gb[:, 0:S - 2], w(0), y[:, 2:S], ALU.mult, ALU.add, t)
                    bput(PB[0], gi, t)
                    t = fn(a_, y, ACT.Silu, t, r0)
                    T.put(i1, t)
                else:
                    t = fn(a_, gb, ACT.Silu, gt, r0)
                    bput(PB[0], gi, t)
                t = tt(dve, a_, a_, ub, ALU.mult, t, ut)
                bput(PB[0], ui, t)
                r = split_out(PH[:, k, :], PL[:, k, :], a_, [t, down[0]])
                T.put(i0, r[1])
                return r

            for half in (0, 1):
                ok = [None] * 11
                i = 11 * half
                if half == 0:
                    ps_ = proj(8, [tag + "g", tag + "u"] * 2, HH, HL, ready)
                    for z in range(2):
                        ok[z] = product(z, 0, ps_[2 * z], ps_[2 * z + 1])
                    i = 2
                while i < 11 * half + 11:
                    ps_ = proj(8, [tag + "g", tag + "u"], HH, HL, ready)
                    ok[i - 11 * half] = product(i, half, ps_[0], ps_[1])
                    i += 1
                if half == 1:
                    hs_pe[0] = [ps_[1][2]]
                for m in range(8):
                    r = proj(11, [tag + "d%d" % half], PH, PL, ok)
                    sink(half, m, r[0])
                    down[0] = [r[0][2]]
            set_table("natural_log_exp_and_others")

        phase_tok = []

        def body():
            W["eng"] = pool
            for m in range(8):
                sq_add(m, X[:, m, :], x_tok[m], SQS)

            set_table("natural_log_exp_and_others")
            S_, t = total_open(SQS)
            for _ in range(15):
                mod_step()
                if M["n"] == 13:
                    mod_sum()
            got = sum_close(S_, 1024, t)
            mod_ready(1)
            for _ in range(SPLIT):
                w_split()

            def first_norm(layer, which, idx, got=None):
                v = 6 * layer + 3 * which
                gain = col(("mix_g", "ffn_g")[which], 8 * layer, 8)
                t = amul(idx, v + 1, gain)
                t2 = mod_ready(v)
                return modulate(MOD[:, v, :], AM[:, idx, :], [t, t2], got)

            def qk_norm(pb, g, dst, gt, done):
                i, b, t = pb
                i0, q, r0 = T.get()
                u = fn(q, b, ACT.Square, t, r0)
                j, sb_, rel = QB[0].get()
                w = mm(sb_, C["blk"][:], q, True, True, rel, u, t_const["blk"], inc=True)
                z = rsqrt_of(sb_, 64, w, q, lambda *a: bput(QB[0], j, *a))
                next(z)
                yield
                k, y, t = next(z)
                T.put(i0, t)
                t = stt(dst, b, g, y, ALU.mult, ALU.mult, t, gt)
                RSR.put(k, t)
                bput(PB[0], i, t)
                done(t)

            NQ = []

            def qk_push(*a):
                z = qk_norm(*a)
                next(z)
                qk_flush()
                NQ.append(z)

            def qk_flush():
                while NQ:
                    for _ in NQ.pop(0):
                        pass

            QB = [None]

            h_ok = first_norm(0, 0, 0, got)
            PB[0] = banks(0, 1, 2, 3, 4, 5)
            LB = banks(6, 7)
            QB[0] = LB
            YH = at("YH", ph, [P, 4, S], F32R)
            YL = at("YL", ph + 8192, [P, 4, S], F32R)
            Q = at("Q", ph + 16384, [P, 4, S])
            K = at("K", ph + 24576, [P, 4, S])
            VV = at("VV", ph + 32768, [P, 4, S])
            XC = at("XC", ph + 40960, [P, 4, S])
            RR = at("RR", ph + 49152, [P, 4, S])
            GI = at("GI", ph + 57344, [P, 4, S])
            GE = at("GE", ph + 65536, [P, 4, S])
            WAX = at("WAX", ph + 73728, [P, 8, 128])
            t_bi = [m_use[15], M["pe"][1]]
            t_wax = sp.dma(WAX[:], wax, s_c[5], 1, t_bi)
            xr, gr = {}, {}
            a_ps = proj(8, ["ev_in"] * 4, HH, HL, h_ok)
            xr[0], gr[0], xr[1], gr[1] = a_ps
            st = {"r": {}, "gi": {}, "ge": {}, "T": {}, "a": {}}

            def lru_front(m):
                i, b, t = xr[m]
                w = lambda j: col("cw", 4 * j + m)
                u = fn(XC[:, m, :], b, ACT.Identity, t, t_bi, bias=col("cb", m), scale=w(3))
                for s_, j in ((1, 2), (2, 1), (3, 0)):
                    u = stt(XC[:, m, s_:S], b[:, 0:S - s_], w(j), XC[:, m, s_:S], ALU.mult, ALU.add, u)
                bput(PB[0], i, u)
                t_xc = u
                i, b, t = gr[m]
                i0, z, r0 = T.get()
                u = fn(z, b, ACT.Square, t, r0)
                u = ts(dve, z, z, 0.044715, 1.0, ALU.mult, ALU.add, u)
                u = tt(dve, z, z, b, ALU.mult, u)
                u = fn(z, z, ACT.Tanh, u, scale=math.sqrt(2.0 / math.pi))
                u = stt(GE[:, m, :], z, 1.0, b, ALU.add, ALU.mult, u, t_bi)
                st["ge"][m] = u
                T.put(i0, u)
                bput(PB[0], i, u)
                yield
                j0, b0, rel0 = LB.get()
                v0 = mm(b0, WAX[:, m, :], XC[:, m, :], True, True, rel0, t_xc, t_wax, inc=True)
                j1, b1, rel1 = LB.get()
                v1 = mm(b1, WAX[:, 4 + m, :], XC[:, m, :], True, True, rel1, inc=True)
                yield
                u0 = fn(RR[:, m, :], b0, ACT.Sigmoid, v0, t_bi, bias=col("ba", m))
                bput(LB, j0, u0)
                i0, z, r0 = T.get()
                u1 = fn(z, b1, ACT.Sigmoid, v1, r0, bias=col("bx", m))
                bput(LB, j1, u1)
                t = tt(dve, GI[:, m, :], z, XC[:, m, :], ALU.mult, u1, t_bi)
                T.put(i0, t)
                st["gi"][m] = t
                st["T"][m] = fn(XC[:, m, :], RR[:, m, :], ACT.Tanh, u0, t, t_cf, scale=CF[:, m:m + 1])

            def lru_back(m):
                u = fn(RR[:, m, :], RR[:, m, :], ACT.Exp, st["T"][m], scale=CF[:, m:m + 1])
                st["a"][m] = u

            def lru_end():
                zt = {}
                for m in range(4):
                    i0, z, r0 = T.get()
                    t = ts(dve, z, XC[:, m, :], -1.0, 1.0, ALU.mult, ALU.add, st["T"][m], r0)
                    t = recip(z, z, t)
                    zt[m] = stt(XC[:, m, :], XC[:, m, :], -2.0, z, ALU.mult, ALU.mult, t)
                    T.put(i0, zt[m])
                    yield
                for m in range(4):
                    zt[m] = fn(XC[:, m, :], XC[:, m, :], ACT.Sqrt, zt[m])
                set_table("natural_log_exp_and_others")
                for m in range(4):
                    z = XC[:, m, :]
                    i1, y, r1 = T.get()
                    t = tt(dve, z, z, GI[:, m, :], ALU.mult, zt[m])
                    t = scan(y, RR[:, m, :], z, t, st["a"][m], r1)
                    t = stt(y, y, 0.5, GE[:, m, :], ALU.mult, ALU.mult, t)
                    r = split_out(YH[:, m, :], YL[:, m, :], y, [t, t_bi])
                    T.put(i1, r[1])
                    ya_ok[m] = r
                    yield

            ya_ok = {}

            q_tok, k_tok, v_tok = {}, {}, {}

            def even_rest():
                vs = proj_rows(8, ["ev_in"] * 4, HH, HL, h_ok)
                for q, (i, b, t) in enumerate(vs):
                    u = fn(VV[:, q, :], b, ACT.Copy, t, t_bi)
                    v_tok[q] = u
                    bput(PB[0], i, u)
                yield

            lf0 = lru_front(0)
            next(lf0)
            lf1 = lru_front(1)
            next(lf1)
            b_ps = proj(8, ["ev_in"] * 4, HH, HL, h_ok)
            xr[2], gr[2], xr[3], gr[3] = b_ps
            for z in (lf0, lf1):
                for _ in z:
                    pass
            lf2, lf3 = lru_front(2), lru_front(3)
            next(lf2)
            next(lf3)
            for _ in even_rest():
                pass
            for z in (lf2, lf3):
                for _ in z:
                    pass
            for m in range(4):
                lru_back(m)
            set_table("natural_log_exp_and_others")
            ends = lru_end()
            M["hold"] = 6
            for m in range(8):
                r = proj(8, ["ev_in"], HH, HL, h_ok)[0]
                next(ends, None)
                if m == 7:
                    hs_pe[0] = [r[2]]
                if m < 4:
                    qk_push(r, QS[:, 0:1], Q[:, m, :], [t_qs, t_bi], lambda t, m=m: q_tok.__setitem__(m, t))
                else:
                    qk_push(r, col("evk"), K[:, m - 4, :], [t_vec, t_bi], lambda t, m=m: k_tok.__setitem__(m - 4, t))
            qk_flush()
            for _ in ends:
                pass
            W["eng"] = dve

            ZB, VB, OB = banks(0, 1, 2, 3), banks(4, 5), banks(6, 7)
            lru_done = [ya_ok[m] for m in range(4)]
            SPB = Ring([at("SPB%d" % i, ph + 40960 + 10240 * i, [P, 1280]) for i in range(3)])
            SNB = Ring([at("SNB%d" % i, ph + 40960 + 10240 * i + 5120, [P, 1280]) for i in range(3)]
                       + [at("SNB3", hh_off, [P, 1280]), at("SNB4", hl_off, [P, 1280])])
            for i in (3, 4):
                SNB.rel[i] = [hs_pe[0]]
            off = [0, 512, 896, 1152]
            wid = [512, 384, 256, 128]
            y_ok = dict(ya_ok)
            ob = {}

            def stick_front(h):
                half = 64 * (h % 2)
                i1, sp_, r1 = SPB.get()
                i2, sn_, r2 = SNB.get()
                toks = {}
                SF[h] = (i1, sp_, i2, sn_, toks)
                for kt in (3, 2, 1, 0):
                    n, o = wid[kt], off[kt]
                    i, b, rel = ZB.get()
                    z = b[:, 0:n]
                    t = mm(z, K[half:half + 64, h // 2, kt * 128:(kt + 1) * 128], Q[half:half + 64, h // 2, S - n:S],
                           True, True, rel, q_tok[h // 2], k_tok[h // 2], inc=True)
                    i0, l, r0 = T.get()
                    l = l[:, 0:n]
                    u = fn(l, z, ACT.Abs, t, r0)
                    u = fn(l, l, ACT.Exp, u, scale=-1.0)
                    u = fn(l, l, ACT.Ln, u, bias=1.0)
                    yield
                    a1 = stt(sp_[:, o:o + n], z, 0.0, l, ALU.max, ALU.add, u, r1, lru_done)
                    a2 = stt(sn_[:, o:o + n], z, 0.0, l, ALU.min, ALU.subtract, r2)
                    bput(ZB, i, a2)
                    T.put(i0, a2)
                    a1 = tt(pool, sp_[:, o:o + 128], sp_[:, o:o + 128], C["tri"][:], ALU.mult, a1, t_const["tri"])
                    toks[kt] = (a1, a2)
                    yield

            def stick_back(h):
                i1, sp_, i2, sn_, toks = SF.pop(h)
                w_t = {}
                SK[h] = (i2, sn_, w_t)
                for kt in (3, 2, 1, 0):
                    n, o = wid[kt], off[kt]
                    i, b, rel = VB.get()
                    last = mm(b[:, 0:n], C["later"][:], sp_[:, o:o + n], True, kt == 3, rel, toks[kt], t_const["later"],
                              inc=(kt == 3))
                    for k2 in range(kt + 1, 4):
                        n2, o2 = wid[k2], off[k2]
                        last = mm(b[:, n - n2:n], C["ones"][:], sp_[:, o2:o2 + n2], False, k2 == 3, toks[k2],
                                  inc=(k2 == 3))
                    if kt == 0:
                        SPB.put(i1, last)
                    w = sn_[:, o:o + n]
                    t = tt(dve, w, w, b[:, 0:n], ALU.subtract, last, toks[kt])
                    bput(VB, i, t)
                    u = fn(w, w, ACT.Exp, t)
                    v = tt(pool, sn_[:, o:o + 128], sn_[:, o:o + 128], C["tri"][:], ALU.mult, u)
                    w_t[kt] = [u, v]
                    yield

            def stick_out(h):
                i2, sn_, w_t = SK.pop(h)
                half = 64 * (h % 2)
                if h % 2 == 0:
                    ob[h // 2] = OB.get()
                j, b, rel = ob[h // 2]
                for kt in range(4):
                    n, o = wid[kt], off[kt]
                    t = mm(b[half:half + 64, S - n:S], VV[:, kt, 64 * h:64 * h + 64], sn_[:, o:o + n], kt == 0, kt == 3,
                           rel, w_t[kt], v_tok[kt], inc=(kt == 3))
                    if kt < 3:
                        yield
                SNB.put(i2, t)
                if h % 2 == 1:
                    m = 4 + h // 2
                    r = split_out(HH[:, m, :], HL[:, m, :], b, [t, hs_pe[0]])
                    bput(OB, j, r)
                    y_ok[m] = r
                yield

            SF, SK = {}, {}
            for _ in stick_front(0):
                pass
            for h in range(10):
                f = stick_front(h + 1) if h + 1 < 8 else iter(())
                b_ = stick_back(h) if h < 8 else iter(())
                o_ = stick_out(h - 1) if 1 <= h < 9 else iter(())
                if M["sum"] is None:
                    mod_step()
                for _ in range(4):
                    next(f, None)
                    next(b_, None)
                    next(o_, None)
                    next(f, None)

            def out_proj(name, ready, gate, t_gate, srcs):
                SQS["sq"] = None
                for m in range(8):
                    got = [PB[0].get()]
                    for k in range(8):
                        b, wh, wl, w_ok, last = next_tiles(1, [name])
                        o = got[0][1]
                        sh, sl, kk = srcs(k)
                        waits = [w_ok, ready[k]] + ([got[0][2]] if k == 0 else [])
                        mm(o, wh, sh[:, kk, :], k == 0, False, waits)
                        mm(o, wh, sl[:, kk, :], False, False)
                        t = mm(o, wl, sh[:, kk, :], False, k == 7, inc=last or k == 7)
                        if last:
                            w_pe[b] = t
                    sink = gate(m, (got[0][0], o, t))
                hs_pe[0] = [t]
                return t

            def add_gated(v):
                def sink(m, pb):
                    tg = mod_ready(v)
                    u = residual(m, pb, MOD[:, v, :], tg, None)
                    sq_add(m, X[:, m, :], u, SQS)
                return sink

            PB[0] = banks(0, 1, 2, 3, 4, 5, 6, 7)
            t_ph = out_proj("ev_out", y_ok, add_gated(2), None,
                            lambda k: (YH, YL, k) if k < 4 else (HH, HL, k))
            phase_tok[:] = [t_ph]

            def guard():
                for q in (act, dve, pool, sp):
                    for w in flat(phase_tok):
                        q.ops.append(([(w[1], w[2])] if q.seen.get(w[0], 0) < w[2] else [], None, 0))
                        q.seen[w[0]] = max(q.seen.get(w[0], 0), w[2])

            guard()

            def first_ffn(layer):
                ready = first_norm(layer, 1, 2 * layer + 1)
                v = 6 * layer + 5

                def sink(half, m, pb):
                    tg = mod_ready(v)
                    u = residual(m, pb, MOD[:, v, :], tg, None)
                    if half == 1:
                        sq_add(m, X[:, m, :], u, SQS)
                        phase_tok[:] = [pb[2]]
                ffn("f%d" % layer, ready, layer, sink)
                guard()

            first_ffn(0)

            h_ok = first_norm(1, 0, 2)
            PB[0] = banks(0, 1, 2, 3, 4, 5)
            QB[0] = banks(6, 7)
            Q2 = at("Q2", ph, [P, 8, S])
            K2 = at("K2", ph + 16384, [P, 2, S])
            V2 = at("V2", ph + 20480, [P, 4, 256])
            PP = Ring([at("PP%d" % i, ph + 24576 + 4096 * i, [P, 4, 256]) for i in range(3)])
            PTS = Ring([at("PTS%d" % i, ph + 36864 + 4096 * i, [P, 2, 512]) for i in range(3)])
            q_tok, k_tok, v_tok = {}, {}, {}
            pend = []

            def odd_sink(m, r):
                if m < 8:
                    qk_push(r, QS[:, 1:2], Q2[:, m, :], t_qs, lambda t: q_tok.__setitem__(m, t))
                else:
                    qk_push(r, col("odk"), K2[:, m - 8, :], t_vec, lambda t: k_tok.__setitem__(m - 8, t))

            for m, r in enumerate(proj(8, ["od_in"] * 4, HH, HL, h_ok)):
                pend.append((m, r))
            for m in range(4, 10):
                r = proj(8, ["od_in"], HH, HL, h_ok)[0]
                pend.append((m, r))
                while len(pend) > (3 if m < 7 else 1):
                    odd_sink(*pend.pop(0))
            while pend:
                odd_sink(*pend.pop(0))
            qk_flush()
            vs = proj_rows(8, ["od_in"] * 2, HH, HL, h_ok)
            hs_pe[0] = [vs[3][2]]
            for q, (i, b, t) in enumerate(vs):
                u = fn(V2[:, q, :], b[:, 0:256], ACT.Copy, t)
                v_tok[q] = u
                bput(PB[0], i, u)

            SB2 = Ring([ps[:, 0:2, :], ps[:, 2:4, :]])
            SB2.rel = [[bankrel[0], bankrel[1]], [bankrel[2], bankrel[3]]]
            PTB = banks(4, 5, 6)
            OB = banks(7)
            smr = Ring([small[:, 16 * i:16 * i + 16] for i in range(4)])
            y_ok = {m: [] for m in range(8)}
            ob = {}

            def swa_front(n, g):
                half = 64 * (g % 2)
                c0 = 0 if n else 1
                i, b, rel = SB2.get()
                sc = b.rearrange("p a (h k) -> p (a h) k", h=2)
                kk = K2[half:half + 64, g // 2, (n - 1 + c0) * 128:(n + 1) * 128]
                for j in range(4):
                    o = sc[:, j, 128 * c0:256]
                    mm(o, Q2[half:half + 64, 4 * (g // 2) + j, n * 128:(n + 1) * 128], kk, True, False,
                       rel, q_tok[4 * (g // 2) + j], k_tok[g // 2])
                    t = mm(o, identr[:], bandr[:, 128 * c0:256], False, True, t_idr, t_bar, inc=(j == 3))
                si, s_, sr = smr.get()
                u = dve.do(lambda e: e.tensor_reduce(s_[:, 0:4], sc[:, :, 128 * c0:256], AX.X, ALU.max), t, sr)
                sk = col("sinks", 4 * g, 4)
                u = tt(dve, s_[:, 0:4], s_[:, 0:4], sk, ALU.max, u)
                t1 = tt(dve, s_[:, 4:8], sk, s_[:, 0:4], ALU.subtract, u)
                u = ts(dve, s_[:, 0:4], s_[:, 0:4], -1.0, None, ALU.mult, None, t1)
                e1 = fn(s_[:, 8:12], s_[:, 4:8], ACT.Exp, t1)
                pi, pp, pr = PP.get()
                for j in range(4):
                    v = fn(pp[:, j, 128 * c0:256], sc[:, j, 128 * c0:256], ACT.Exp, u, pr,
                           bias=s_[:, j:j + 1], acc=s_[:, 12 + j:13 + j])
                SB2.put(i, v)
                for q in range(2):
                    bankrel[2 * i + q] = [v]
                return n, g, c0, pi, pp, si, s_, [v, e1]

            def swa_scale(f):
                n, g, c0, pi, pp, si, s_, tok = f
                w = tt(dve, s_[:, 12:16], s_[:, 12:16], s_[:, 8:12], ALU.add, tok)
                w = recip(s_[:, 12:16], s_[:, 12:16], w)
                for j in range(4):
                    w2 = ts(dve, pp[:, j, 128 * c0:256], pp[:, j, 128 * c0:256], s_[:, 12 + j:13 + j], None, ALU.mult, None, w)
                smr.put(si, w2)
                return n, g, c0, pi, pp, w2

            def swa_back(f):
                n, g, c0, pi, pp, tok = f
                half = 64 * (g % 2)
                xi, px, xr_ = PTS.get()
                cps = {}
                for c in range(c0, 2):
                    i, b, rel = PTB.get()
                    for j in range(4):
                        t = tpose(b[:, j * 128:(j + 1) * 128], pp[:, j, c * 128:(c + 1) * 128], C["ident"][:],
                                  rel, tok, t_const["ident"], inc=(j == 3))
                    cps[c] = fn(px[:, c, :], b, ACT.Copy, t, xr_) if c == 0 else cp(dve, px[:, c, :], b, t, xr_)
                    bput(PTB, i, cps[c])
                PP.put(pi, t)
                return n, g, c0, xi, px, cps

            def swa_out(f):
                n, g, c0, xi, px, cps = f
                half = 64 * (g % 2)
                key = (n, g // 2)
                if g % 2 == 0:
                    ob[key] = OB.get()
                j, b, rel = ob[key]
                for c in range(c0, 2):
                    t = mm(b[half:half + 64, :], V2[:, n - 1 + c, 64 * g:64 * g + 64], px[:, c, :], c == c0, c == 1,
                           rel, cps[c], v_tok[n - 1 + c], inc=(c == 1))
                PTS.put(xi, t)
                if g % 2 == 1:
                    a_ = 4 * (g // 2)
                    src = b.rearrange("p (j q) -> p j q", j=4)
                    r = split_out(HH[:, a_:a_ + 4, n * 128:(n + 1) * 128], HL[:, a_:a_ + 4, n * 128:(n + 1) * 128],
                                  src, [t, hs_pe[0]])
                    bput(OB, j, r)
                    for m in range(a_, a_ + 4):
                        y_ok[m].append(r)

            OH = at("OH", ph + 49152, [33, 704])
            TB = at("TB", ph + 52096, [33, 48])
            FV = at("FV", ph + 52352, [16, 704])
            FLIP = at("FLIP", ph + 55296, [P, P])
            TR = Ring([at("TR%d" % i, ph + 56320 + 2048 * i, [P, 4, 128]) for i in range(4)])
            ST = Ring([at("ST%d" % i, ph + 64512 + 2048 * i, [P, 4, 128]) for i in range(2)])
            t_oh = sp.dma(OH[:], oh, s_c[2], 1, phase_tok)
            t_neg = pool.do(lambda e: e.memset(TB[32:33, :], NEG))
            t_tab = sp.dma(TB[0:32, :], tab, s_c[3], 1, phase_tok)
            t_flip = sp.dma(FLIP[:], flip, s_c[4], 1, phase_tok)
            s_tr = [sem("s_tr%d" % i) for i in range(4)]
            s_st = [sem("s_st%d" % i) for i in range(13)]
            s_fv = sem("s_fv")
            B["stored"] = []

            def bias_tables():
                toks = []
                for g, a, w in ((2, 0, 64), (1, 64, 256), (0, 320, 384)):
                    i, b, rel = PTB.get()
                    t = mm(b[0:16, 0:w], TB[:, 16 * g:16 * g + 16], OH[:, a:a + w], True, True, rel, t_oh, t_tab, t_neg,
                           inc=True)
                    toks.append(fn(FV[:, a:a + w], b[0:16, 0:w], ACT.Copy, t))
                    bput(PTB, i, toks[-1])
                B["fv"] = sp.dma(bvec, FV[:], s_fv, 1, toks)
                yield
                units = [(h0, nh, at_, nk, src) for at_, nk, src in
                         ((0, 128, 321), (128, 128, 449), (256, 128, 65)) for h0, nh in ((0, 4), (4, 4), (8, 4), (12, 4))]
                units.append((0, 16, 384, 32, 1))
                loads = {}

                def load(n):
                    h0, nh, at_, nk, src = units[n]
                    ri, r_, rr = TR.get()
                    r_ = r_.rearrange("p a k -> p (a k)").rearrange("p (h k) -> p h k", h=nh)
                    for z in range(4 if nh == 16 else 1):
                        np_ = 32 if nh == 16 else P
                        view = bass.AP(bvec.tensor, bvec.offset + 704 * h0 + src, [[1, np_], [704, nh], [1, nk]])
                        t = sp.dma(r_[np_ * z:np_ * z + np_], view, s_tr[ri], n // 4 + 1 + z, rr, B["fv"])
                    loads[n] = (ri, r_, t)

                for n in range(3):
                    load(n)
                yield
                for n, (h0, nh, at_, nk, src) in enumerate(units):
                    if n + 3 < len(units):
                        load(n + 3)
                    ri, r_, t = loads[n]
                    i, b, rel = PTB.get()
                    t = mm(b, FLIP[:], r_.rearrange("p h k -> p (h k)"), True, True, rel, t, t_flip, inc=True)
                    TR.put(ri, t)
                    si, st_, sr = ST.get()
                    u = fn(st_[:].rearrange("p a k -> p (a k)"), b, ACT.Copy, t, sr)
                    bput(PTB, i, u)
                    t = sp.dma(scratch[:, h0:h0 + nh, at_:at_ + nk],
                               st_[:].rearrange("p a k -> p (a k)").rearrange("p (h k) -> p h k", h=nh), s_st[n], 1, u)
                    ST.put(si, t)
                    B["stored"].append(t)
                    yield

            g_bias = bias_tables()
            units = [(n, g) for n in range(4) for g in range(4)]
            fr, sc_, mid = [], [], []
            for x_ in units + [None] * 3:
                if x_:
                    fr.append(swa_front(*x_))
                if fr and (len(fr) > 1 or not x_):
                    sc_.append(swa_scale(fr.pop(0)))
                next(g_bias, None)
                if mid:
                    swa_out(mid.pop(0))
                if sc_ and (len(sc_) > 1 or not x_):
                    mid.append(swa_back(sc_.pop(0)))
            assert not (fr or sc_)
            while mid:
                swa_out(mid.pop(0))
            for _ in g_bias:
                pass
            phase_tok[:] = B["stored"]
            PB[0] = banks(0, 1, 2, 3, 4, 5, 6, 7)
            t_ph = out_proj("od_out", y_ok, add_gated(8), None, lambda k: (HH, HL, k))
            phase_tok[:] = [t_ph] + B["stored"]
            guard()
            first_ffn(1)

            def pre_norm(layer, sub):
                v = 12 + 9 * layer + 3 * sub
                idx = 4 + 3 * layer + sub
                t = amul(idx, v + 1, col("pre", 24 * layer + 8 * sub, 8))
                t2 = mod_ready(v)
                got = None
                if NX.get("got"):
                    got = sum_close(NX["got"][0], 1024, NX["got"][1])
                    NX["got"] = None
                return modulate(MOD[:, v, :], AM[:, idx, :], [t, t2], got)

            YS = {"tok": [None] * 8}

            def y_store(Y, m, pb, half, st2):
                i, b, t = pb
                if half == 0:
                    u = fn(Y[:, m, :], b, ACT.Copy, t)
                    YS["tok"][m] = u
                    bput(PB[0], i, u)
                    return
                if half == 1:
                    u = tt(dve, Y[:, m, :], b, Y[:, m, :], ALU.add, t, YS["tok"][m])
                else:
                    u = cp(dve, Y[:, m, :], b, t)
                YS["tok"][m] = u
                bput(PB[0], i, u)
                sq_add(m, Y[:, m, :], u, SQS)
                YS["sq"] = [SQS["sq"], SQS["last"][2] if m == 7 else None]

            def post_norm(Y, layer, sub, last=False):
                v = 12 + 9 * layer + 3 * sub + 2
                idx = 3 * layer + sub
                tg = mod_ready(v)
                t0 = stt(GM[:, idx, :], MOD[:, v, :], (0.5, 1.0, 0.5)[sub], col("post", 24 * layer + 8 * sub, 8),
                         ALU.mult, ALU.mult, tg, t_vec)
                j, R, tr = total(SQS, 1024)
                S_ = None if last else sum_open()

                def square(m):
                    i0, z, r0 = T.get()
                    u = fn(z, X[:, m, :], ACT.Square, x_tok[m], r0)
                    w = sum_add(S_, z, u, m == 7)
                    T.put(i0, w)
                    return w

                prev = None
                for m in range(8):
                    t = stt(Y[:, m, :], Y[:, m, :], GM[:, idx, m:m + 1], R, ALU.mult, ALU.mult, tr, t0, YS["tok"][m],
                            YS["sq"])
                    if m in (0, 2, 4):
                        x_tok[m] = tt(pool, X[:, m, :], X[:, m, :], Y[:, m, :], ALU.add, t, x_tok[m])
                    else:
                        if prev is not None:
                            x_tok[prev[0]] = tt(dve, X[:, prev[0], :], X[:, prev[0], :], Y[:, prev[0], :], ALU.add,
                                                prev[1], x_tok[prev[0]])
                        prev = (m, t)
                x_tok[prev[0]] = tt(dve, X[:, prev[0], :], X[:, prev[0], :], Y[:, prev[0], :], ALU.add,
                                    prev[1], x_tok[prev[0]])
                RSR.put(j, t)
                phase_tok[:] = list(x_tok)
                if not last:
                    for m in range(8):
                        w = square(m)
                    NX["got"] = (S_, w)
                guard()

            NX = {}

            def second_ffn(layer, which):
                sub = 2 * which
                ready = pre_norm(layer, sub)
                tag = "ab"[layer] + str(which)
                Y = at("Y" + tag, ph + 45056, [P, 8, S])
                ffn(tag, ready, None, lambda half, m, pb: y_store(Y, m, pb, half, None))
                post_norm(Y, layer, sub, last=(layer == 1 and which == 1))

            second_ffn(0, 0)

            h_ok = pre_norm(0, 1)
            PB[0] = banks(0, 1, 2, 3, 4, 5)
            CL = at("CL", ph, [P, 5, S])
            CH = at("CH", ph + 10240, [P, 5, S], F32R)
            CW = at("CW", ph + 20480, [P, 5, S], F32R)
            VM = at("VM", ph + 30720, [P, 4, 1024])
            TG = at("TG", ph + 47104, [P, S])
            KRP = at("KRP", ph + 49152, [P, S])
            QH = Ring([at("QH%d" % i, ph + 51200 + 2048 * i, [P, S]) for i in range(3)])
            KH = Ring([at("KH%d" % i, ph + 57344 + 2048 * i, [P, S]) for i in range(3)])
            PM = Ring([at("PM%d" % i, ph + 63488 + 2048 * i, [P, S]) for i in range(4)])
            PTM = Ring([at("PTM%d" % i, ph + 71680 + 2048 * i, [P, S]) for i in range(3)])
            t_trig = sp.dma(TG[:], trig, s_c[6], 1)
            lat = proj(8, ["mla_in"] * 6, HH, HL, h_ok)
            hs_pe[0] = [lat[5][2]]
            SBQ = banks(6, 7)

            def lat_norm(tiles_, n, gname, out0):
                i, b, rel = SBQ.get()
                cpt = []
                for k, m in enumerate(tiles_):
                    bi, bk, bt = lat[m]
                    i0, z, r0 = T.get()
                    u = fn(z, bk, ACT.Square, bt, r0)
                    w = mm(b, C["ones"][:], z, k == 0, k == len(tiles_) - 1, rel, u, inc=True)
                    T.put(i0, w)
                    c = cp(dve, CL[:, m, :], bk, bt, u)
                    bput(PB[0], bi, c, u)
                    cpt.append(c)
                i0, q, r0 = PM.get()
                z = rsqrt_of(b, n, [w, r0], q[:], lambda *a: bput(SBQ, i, *a))
                next(z)
                yield
                j, R, tr = next(z)
                PM.put(i0, tr)
                for k, m in enumerate(tiles_):
                    t = stt(CL[:, m, :], CL[:, m, :], col(gname, k), R, ALU.mult, ALU.mult, tr, cpt[k])
                    c_ok[m] = split_out(CH[:, m, :], CW[:, m, :], CL[:, m, :], t)
                RSR.put(j, t)
                yield

            c_ok = {}
            norms = [lat_norm([3, 4], 256, "mkv", 3), lat_norm([0, 1, 2], 384, "mq", 0)]
            for _ in range(2):
                for z in norms:
                    next(z)

            def rope(dst, b, t, extra):
                i0, z, r0 = T.get()
                t1 = tt(dve, dst, b[64:96, :], TG[64:96, :], ALU.mult, t, t_trig, extra)
                t2 = tt(dve, z[64:96, :], b[96:128, :], TG[96:128, :], ALU.mult, t, r0)
                t3 = tt(pool, dst, dst, z[64:96, :], ALU.add, t1, t2)
                T.put(i0, t3)
                return t3, t2

            bi, bk, bt = lat[5]
            t_kr, tb_ = rope(KRP[64:96, :], bk, bt, [])
            bput(PB[0], bi, tb_)
            vm_tok = {}
            for f in range(2):
                vs = proj_rows(2, ["mla_v"] * 4, CH[:, 3:5, :], CW[:, 3:5, :], {0: c_ok[3], 1: c_ok[4]})
                for q, (i, b, t) in enumerate(vs):
                    u = fn(VM[:, q, 512 * f:512 * f + 512], b, ACT.Copy, t)
                    vm_tok[(q, f)] = u
                    bput(PB[0], i, u)
            PB[0] = banks(6, 7)
            SM = banks(0, 1, 2)
            PTB = banks(3, 4)
            OB = banks(5)
            MH = {}
            kbank = {}

            def mla_proj(h):
                i, b, t = proj(3, ["mla_q"], CH, CW, c_ok)[0]
                qi, q, qr = QH.get()
                u1 = fn(q[0:64, :], b[0:64, :], ACT.Copy, t, qr)
                u2, u3 = rope(q[64:96, :], b, t, qr)
                bput(PB[0], i, u1, u3)
                yield
                if h % 2 == 0:
                    i, b, t = proj(2, ["mla_k"], CH, CW, c_ok, k0=3)[0]
                    kt_ = []
                    for z in range(2):
                        ki, k, kr = KH.get()
                        w1 = fn(k[0:64, :], b[64 * z:64 * z + 64, :], ACT.Copy, t, kr)
                        w2 = pool.do(lambda e, k=k: e.tensor_copy(k[64:96, :], KRP[64:96, :]), t_kr, kr)
                        kbank[h + z] = (ki, k, [w1, w2])
                    bput(PB[0], i, w1)
                MH[h] = (qi, q, [u1, u2]) + kbank[h]
                yield

            def mla_front(h, n):
                qi, q, qt, ki, k, kt_ = MH[h]
                w = 128 * (n + 1)
                i, b, rel = SM.get()
                mm(b[:, 0:w], q[0:96, n * 128:(n + 1) * 128], k[0:96, 0:w], True, False, rel, qt, kt_)
                t = mm(b[:, w - 128:w], identr[:], causr[:], False, True, t_idr, t_car, inc=True)
                if n == 3:
                    QH.put(qi, t)
                    KH.put(ki, t)
                si, s_, sr = smr.get()
                u = dve.do(lambda e: e.tensor_reduce(s_[:, 0:1], b[:, 0:w], AX.X, ALU.max), t, sr)
                u = ts(dve, s_[:, 0:1], s_[:, 0:1], -MLA_SCALE, None, ALU.mult, None, u)
                pi, pp, pr = PM.get()
                v = fn(pp[:, 0:w], b[:, 0:w], ACT.Exp, u, pr, bias=s_[:, 0:1], scale=MLA_SCALE, acc=s_[:, 1:2])
                bput(SM, i, v)
                x_ = recip(s_[:, 1:2], s_[:, 1:2], v)
                x_ = ts(dve, pp[:, 0:w], pp[:, 0:w], s_[:, 1:2], None, ALU.mult, None, x_)
                smr.put(si, x_)
                return h, n, pi, pp, x_

            def mla_mid(f):
                h, n, pi, pp, tok = f
                w = 128 * (n + 1)
                i, b, rel = PTB.get()
                for c in range(n + 1):
                    t = tpose(b[:, c * 128:(c + 1) * 128], pp[:, c * 128:(c + 1) * 128], C["ident"][:], rel, tok,
                              inc=(c == n))
                PM.put(pi, t)
                xi, px, xr_ = PTM.get()
                u = fn(px[:, 0:w], b[:, 0:w], ACT.Copy, t, xr_) if n % 2 else cp(dve, px[:, 0:w], b[:, 0:w], t, xr_)
                bput(PTB, i, u)
                return h, n, xi, px, u

            def mla_out(f):
                h, n, xi, px, u = f
                half = 64 * (h % 2)
                if n == 0 and h % 2 == 0:
                    ob[h // 2] = OB.get()
                j, ob_, orel = ob[h // 2]
                for c in range(n + 1):
                    t = mm(ob_[half:half + 64, n * 128:(n + 1) * 128], VM[:, c, 64 * h:64 * h + 64],
                           px[:, c * 128:(c + 1) * 128], c == 0, c == n, orel, u, vm_tok[(c, h // 8)], inc=(c == n))
                PTM.put(xi, t)
                if h % 2 == 1 and n == 3:
                    m = h // 2
                    r = split_out(HH[:, m, :], HL[:, m, :], ob_, [t, hs_pe[0]])
                    bput(OB, j, r)
                    y_ok[m] = r

            def mla_steps():
                fr, mid = [], []
                for x_ in [(h, n) for h in range(16) for n in range(4)] + [None] * 4:
                    if x_:
                        fr.append(mla_front(*x_))
                    if len(fr) > 2 or (fr and not x_):
                        mid.append(mla_mid(fr.pop(0)))
                    if len(mid) > 1 or (mid and not x_):
                        mla_out(mid.pop(0))
                    yield x_
                while mid:
                    mla_out(mid.pop(0))

            y_ok = {}
            for _ in mla_proj(0):
                pass
            side = None
            steps = mla_steps()
            for h in range(16):
                side = mla_proj(h + 1) if h < 15 else iter(())
                for n in range(4):
                    next(steps)
                    if n < 3:
                        next(side, None)
            for _ in steps:
                pass
            PB[0] = banks(0, 1, 2, 3, 4, 5, 6, 7)
            phase_tok[:] = [y_ok[7]]
            guard()
            Y = at("Ymla", ph + 45056, [P, 8, S])
            t_ph = out_proj("mla_o", y_ok, lambda m, pb: y_store(Y, m, pb, 2, None), None, lambda k: (HH, HL, k))
            post_norm(Y, 0, 1)
            second_ffn(0, 1)
            second_ffn(1, 0)

            h_ok = pre_norm(1, 1)
            mod_ready(29)
            mod_done = [m_tok[29], m_use[239]]
            PB[0] = banks(0, 1, 2, 3)
            YF = at("YF", ph, [P, 8, S])
            QK = Ring([at("QK%d" % i, ph + 16384 + 12288 * i, [P, 6, S]) for i in range(2)])
            VT = at("VT", ph + 40960, [P, 3, S])
            VN = Ring([at("VN%d" % i, ph + 47104 + 6144 * i, [P, 12, 128]) for i in range(2)])
            SD = Ring([at("SD%d" % i, ph + 59392 + 6144 * i, [P, 1536]) for i in range(2)])
            PD = at("PD", ph + 71680, [P, 1408])
            BB = Ring([at("BB%d" % i, macc_off - 8192 + 4096 * i, [P, 2, 416]) for i in range(2)])
            RB = at("RB", macc_off, [P, 4, 4, 32])
            s_bb = [sem("s_bb%d" % i) for i in range(2)]
            mrow = at("mrow", macc_off + 2048, [2, S])
            vt_rel, dl = [[]], {}
            pool_b = banks(4, 5, 6, 7)
            first4 = proj(8, ["dil_in"] * 4, HH, HL, h_ok)

            def tok_view(ap, g, j):
                if g == 0:
                    return ap[:, 128 * j:128 * j + 128]
                if g == 1:
                    return ap.rearrange("p (i r) -> p r i", r=4)[:, j, :]
                return ap.rearrange("p (k a j) -> p j a k", k=32, a=4)[:, j, :, :]

            def dil_proj(c):
                qi, qk, qr = QK.get()
                vi, vn, vr = VN.get()
                bi_, bb, br = BB.get()
                t_bb = sp.dma(bb[:], scratch[:, 2 * c:2 * c + 2, :], s_bb[c % 2], c // 2 + 1, br, mod_done, B["stored"])
                toks = {}
                for g in range(3):
                    for t_ in range(3):
                        n = 3 * g + t_
                        if c == 0 and n < 4:
                            i, b, t = first4[n]
                        else:
                            i, b, t = proj(8, ["dil_in"], HH, HL, h_ok)[0]
                        if t_ == 0:
                            u = fn(qk[:, 2 * g, :], b, ACT.Copy, t, qr, scale=0.125)
                            toks[(g, 0)] = u
                            bput(PB[0], i, u)
                        elif t_ == 1:
                            u = cp(dve, qk[:, 2 * g + 1, :], b, t, qr)
                            toks[(g, 1)] = u
                            bput(PB[0], i, u)
                        else:
                            if g == 2:
                                u = fn(VT[:, 2, :].rearrange("p (j a k) -> p j a k", j=4, a=4),
                                       b.rearrange("p (k a j) -> p j a k", k=32, a=4), ACT.Copy, t, vt_rel[0])
                            else:
                                u = fn(VT[:, g, :], b, ACT.Copy, t, vt_rel[0])
                            bput(PB[0], i, u)
                            i, b, rel = PB[0].get()
                            for j in range(4):
                                t = tpose(b[:, 128 * j:128 * j + 128], tok_view(VT[:, g, :], g % 2, j), C["ident"][:], rel, u,
                                          inc=(j == 3))
                            u = cp(dve, vn[:, 4 * g:4 * g + 4, :], b.rearrange("p (j f) -> p j f", j=4), t, vr)
                            toks[(g, 2)] = u
                            bput(PB[0], i, u)
                            vtl.append(t)
                            vt_rel[0] = []
                        if n % 3 == 2 and g == 2:
                            vt_rel[0] = list(vtl)
                            vtl.clear()
                        yield
                hs_pe[0] = [t]
                dl[c] = (qi, qk, vi, vn, bi_, bb, t_bb, toks)

            vtl = []

            def dil_att(c):
                qi, qk, vi, vn, bi_, bb, t_bb, toks = dl[c]
                cm = small[:, 64:88].rearrange("p (j h) -> p j h", h=2)
                cn = small[:, 88:112].rearrange("p (j h) -> p j h", h=2)
                cs = small[:, 112:136].rearrange("p (j h) -> p j h", h=2)
                sds = []
                maxes = []
                g0off = [0, 128, 384, 640]
                g0wid = [128, 256, 256, 256]
                for hh in range(2):
                    half = 64 * hh
                    di, sd, dr = SD.get()
                    bk = [pool_b.get() for _ in range(4)]
                    hsl = slice(half, half + 64)
                    place = {}
                    for n in range(4):
                        b = bk[n // 2]
                        o = (0, 128)[n] if n < 2 else (0, 256)[n - 2]
                        w = g0wid[n]
                        ap = b[1][:, o:o + w]
                        t = mm(ap, qk[hsl, 0, n * 128:(n + 1) * 128], qk[hsl, 1, (n + 1) * 128 - w:(n + 1) * 128], True, True,
                               b[2], toks[(0, 0)], toks[(0, 1)], inc=True)
                        place[n] = (ap, bb[:, hh, 256 - w:256], sd[:, g0off[n]:g0off[n] + w], t)
                    for r in range(4):
                        b = bk[2]
                        ap = b[1][:, 128 * r:128 * r + 128]
                        t = mm(ap, tok_view(qk[hsl, 2, :], 1, r), tok_view(qk[hsl, 3, :], 1, r), True, True, b[2],
                               toks[(1, 0)], toks[(1, 1)], inc=True)
                        place[4 + r] = (ap, bb[:, hh, 256:384], sd[:, 896 + 128 * r:1024 + 128 * r], t)
                    b = bk[3]
                    for a_ in range(4):
                        for j in range(4):
                            r = 4 * a_ + j
                            t = mm(b[1][32 * j:32 * j + 32, 32 * a_:32 * a_ + 32], qk[hsl, 4, r:S:16], qk[hsl, 5, r:S:16],
                                   True, True, b[2], toks[(2, 0)], toks[(2, 1)], inc=(j == 3))
                        place[8 + a_] = (b[1][:, 32 * a_:32 * a_ + 32], bb[:, hh, 384:416],
                                         sd[:, 1408 + 32 * a_:1440 + 32 * a_], t)
                    for s_ in range(12):
                        ap, bias, dst, _ = place[s_]
                        t = place[(1, 3, 7, 11)[s_ // 2 if s_ < 4 else (2 if s_ < 8 else 3)]][3]
                        u = dve.do(lambda e, ap=ap, bias=bias, dst=dst, s_=s_, hh=hh: e.tensor_tensor_reduce(
                            out=dst, in0=ap, in1=bias, scale=1.0, scalar=-3.0e38, op0=ALU.add, op1=ALU.max,
                            accum_out=cm[:, s_, hh:hh + 1]), t, t_bb, dr, cmr[0])
                        q = s_ // 2 if s_ < 4 else (2 if s_ < 8 else 3)
                        bput(pool_b, bk[q][0], u)
                    maxes.append(u)
                    sds.append((di, sd, place))
                    yield
                BB.put(bi_, u)
                QK.put(qi, t)
                i, b, rel = pool_b.get()
                for s_ in range(12):
                    g, j = s_ // 4, s_ % 4
                    o = tok_view(b[32 * g:32 * g + 2, :], g, j)
                    if g == 2:
                        o = b[64:66, :].rearrange("p (i a j) -> p a j i", i=32, a=4)[:, j, :, :]
                    t = mm(o, cm[:, s_, :], C["ident"][:], True, True, rel, maxes, inc=(s_ == 11))
                u = cp(dve, mrow[:], b[0:2, :], t, mrel[0], mod_done)
                u = tt(dve, mrow[:], mrow[:], b[32:34, :], ALU.max, u)
                u = tt(dve, mrow[:], mrow[:], b[64:66, :], ALU.max, u)
                cmr[0] = [t]
                bput(pool_b, i, u)
                yield
                i, b, rel = pool_b.get()
                for s_ in range(12):
                    g, j = s_ // 4, s_ % 4
                    o = b[:, 2 * s_:2 * s_ + 2]
                    if g < 2:
                        mm(o, tok_view(mrow[:], g, j), C["ident"][0:2, 0:2], True, True, rel, u)
                        continue
                    for z in range(4):
                        t = mm(o[32 * z:32 * z + 32, :], mrow[:, 4 * j + z:S:16], C["ident"][0:2, 0:2], True, True,
                               inc=(s_ == 11 and z == 3))
                mrel[0] = [t]
                un = ts(dve, cn, b[:, 0:24].rearrange("p (j h) -> p j h", h=2), -1.0, None, ALU.mult, None, t, cnr[0])
                bput(pool_b, i, un)
                yield
                exps = []
                for hh in range(2):
                    di, sd, place = sds[hh]
                    for s_ in range(12):
                        dst = place[s_][2]
                        v = fn(dst, dst, ACT.Exp, un, maxes[hh], csr[0], bias=cn[:, s_, hh:hh + 1], acc=cs[:, s_, hh:hh + 1])
                    exps.append(v)
                cnr[0] = [v]
                yield
                i, b, rel = pool_b.get()
                for s_ in range(12):
                    g, j = s_ // 4, s_ % 4
                    o = tok_view(b[0:2, :], g, j)
                    if g == 2:
                        o = b[0:2, :].rearrange("p (i a j) -> p a j i", i=32, a=4)[:, j, :, :]
                    t = mm(o, cs[:, s_, :], C["ident"][:], s_ == 0, s_ == 11, rel, exps, inc=(s_ == 11), skip=True)
                csr[0] = [t]
                u = recip(mrow[:], b[0:2, :], t, mrel[0])
                bput(pool_b, i, u)
                oi, o_, orel = OBD.get()
                for hh in range(2):
                    di, sd, place = sds[hh]
                    half = 64 * hh
                    cpt = {}
                    srcs = [sd[:, 128 * z:128 * z + 128] for z in range(12)]
                    for z3 in range(3):
                        i, b, rel = pool_b.get()
                        for z in range(4):
                            t = tpose(b[:, 128 * z:128 * z + 128], srcs[4 * z3 + z], C["ident"][:], rel, exps[hh],
                                      inc=(z == 3))
                        if z3 < 2:
                            cpt[z3] = fn(PD[:, 512 * z3:512 * z3 + 512], b, ACT.Copy, t, pdr[0])
                            bput(pool_b, i, cpt[z3])
                        else:
                            v1 = fn(PD[:, 1024:1408], b[:, 0:384], ACT.Copy, t, pdr[0])
                            vv = []
                            for a_ in range(4):
                                vv.append(ts(dve, RB[:, :, a_, :], b[:, 384:512].rearrange("p (j i) -> p j i", j=4),
                                             C["adiag"][:, a_:a_ + 1], None, ALU.mult, None, t, v1, pdr[0], mod_done))
                            cpt[2] = [v1] + vv
                            bput(pool_b, i, v1, vv)
                    SD.put(di, t)
                    blk = 0
                    oh_ = o_[half:half + 64, :]
                    fs = slice(64 * hh, 64 * hh + 64)
                    for n in range(4):
                        for c_ in ((1,) if n == 0 else (0, 1)):
                            t = mm(oh_[:, n * 128:(n + 1) * 128], vn[:, n - 1 + c_, fs], PD[:, 128 * blk:128 * blk + 128],
                                   blk == 0, False, orel, cpt[blk // 4], toks[(0, 2)], skip=True)
                            blk += 1
                    for r in range(4):
                        mm(tok_view(oh_, 1, r), vn[:, 4 + r, fs], PD[:, 128 * blk:128 * blk + 128], False, False,
                           cpt[blk // 4], toks[(1, 2)], skip=True)
                        blk += 1
                    for j in range(4):
                        o = oh_.rearrange("p (i a j) -> p j a i", i=32, a=4)[:, j, :, :]
                        t = mm(o, vn[:, 8 + j, fs], RB[:, j, :, :], False, j == 3, cpt[2], toks[(2, 2)], inc=(j == 3), skip=True)
                    pdr[0] = [t]
                    yield
                VN.put(vi, t)
                i, b, rel = pool_b.get()
                t2 = mm(b, C["sel"][0:2, :], mrow[:], True, True, rel, u, t_const["sel"], inc=True)
                mrel[0] = [t2]
                i0, z, r0 = T.get()
                u = fn(z, b, ACT.Copy, t2, r0)
                bput(pool_b, i, u)
                u = tt(dve, YF[:, c, :], z, o_, ALU.mult, u, t)
                bput(OBD, oi, u)
                T.put(i0, u)
                yf_tok[c] = u
                yield

            cmr, cnr, csr, mrel, pdr, yf_tok = [[]], [[]], [[]], [[]], [[]], {}
            gp = dil_proj(0)
            for _ in range(4):
                next(gp)
            PBX = banks(0, 1, 2)
            PB[0] = PBX
            OBD = banks(3)
            for _ in gp:
                pass
            for c in range(8):
                if c < 7:
                    weave(dil_proj(c + 1), dil_att(c), 1)
                else:
                    y_ok = {}
                    at_ = dil_att(c)
                    next(at_)
                    next(at_)
                    for m in range(7):
                        y_ok[m] = split_out(HH[:, m, :], HL[:, m, :], YF[:, m, :], [yf_tok[m], hs_pe[0]])
                        next(at_, None)
                    for _ in at_:
                        pass
            PB[0] = banks(0, 1, 2, 3, 4, 5, 6, 7)
            y_ok[7] = split_out(HH[:, 7, :], HL[:, 7, :], YF[:, 7, :], yf_tok[7])
            phase_tok[:] = [y_ok[m] for m in range(8)]
            guard()
            Y = at("Ydil", ph + 45056, [P, 8, S])
            out_proj("dil_o", y_ok, lambda m, pb: y_store(Y, m, pb, 2, None), None, lambda k: (HH, HL, k))
            post_norm(Y, 1, 1)
            second_ffn(1, 1)
            assert W["tile"] == len(tiles)
            return sp.dma(out, X[:], s_c[7], 1, x_tok)
        t_out = body()

        block = ctx.enter_context(nc.Block())

        def play(q, eng, extra=()):
            pend_ = []
            for need, f, inc in q.ops:
                for s_, v in need:
                    eng.wait_ge(s_, v)
                if f is None:
                    continue
                ins = f(eng)
                if inc:
                    ins.then_inc(q.sem, 1)
            for w in extra:
                eng.wait_ge(w[1], w[2])

        @block.sync
        def _(e):
            play(sp, e, B.get("stored", []) + [t_out])

        @block.scalar
        def _(e):
            play(act, e)

        @block.vector
        def _(e):
            play(dve, e)

        @block.gpsimd
        def _(e):
            play(pool, e)

        @block.tensor
        def _(e):
            play(pe, e)


def matrices(a):
    m = {}
    ev = a["ev_w_in"][0]
    m["ev_in"] = ev
    m["ev_out"] = a["ev_w_out"][0]
    od = a["od_w_in"][0]
    order = [h for t in range(2) for j in range(4) for h in (8 * t + j, 8 * t + 4 + j)]
    q = od[:, :1024].reshape(1024, 16, 64)[:, order].reshape(1024, 1024)
    m["od_in"] = np.concatenate([q, od[:, 1024:]], axis=1)
    m["od_out"] = a["od_w_out"][0].reshape(16, 64, 1024)[order].reshape(1024, 1024)
    for l in range(2):
        m["f%dg" % l] = a["ffn_w_gate"][l]
        m["f%du" % l] = a["ffn_w_up"][l]
        for half in range(2):
            m["f%dd%d" % (l, half)] = a["ffn_w_down"][l][1408 * half:1408 * half + 1408]
    for l in range(2):
        for w in range(2):
            t = "ab"[l] + str(w)
            m[t + "g"] = a["ffn_w_gate_2"][l, w]
            m[t + "u"] = a["ffn_w_up_2"][l, w]
            for half in range(2):
                m[t + "d%d" % half] = a["ffn_w_down_2"][l, w][1408 * half:1408 * half + 1408]
    wi = a["mla_w_in_2"][0]
    kr = wi[:, 640:672]
    sw = np.concatenate([kr[:, 16:], kr[:, :16]], axis=1)
    m["mla_in"] = np.concatenate([wi[:, :640], kr, kr, kr, sw], axis=1)
    qu = a["mla_w_q_up_2"][0].reshape(384, 16, 96)
    m["mla_q"] = np.concatenate([qu, qu[:, :, 80:96], qu[:, :, 64:80]], axis=2).reshape(384, 2048)
    kv = a["mla_w_kv_up_2"][0].reshape(256, 16, 128)
    m["mla_k"] = kv[:, :, :64].reshape(256, 1024)
    m["mla_v"] = kv[:, :, 64:].reshape(256, 1024)
    m["mla_o"] = a["mla_w_o_2"][0]
    m["dil_in"] = a["dil_w_in_2"][0]
    m["dil_o"] = a["dil_w_o_2"][0]
    return m


def pack_stream(a):
    m = matrices(a)
    tiles = tile_list()
    nb = (len(tiles) + BT - 1) // BT
    out = np.zeros((nb, P, BT * 128), np.float32)
    for t, (name, k, c) in enumerate(tiles):
        b, o = divmod(t, BT)
        out[b, :, o * 128:(o + 1) * 128] = m[name][k * 128:(k + 1) * 128, c * 128:(c + 1) * 128]
    return out


def pack_mod(a):
    out = np.empty((240, P, 1024), np.float32)
    n = 0
    for w, nv in ((a["ada_w"], 6), (a["w_mod_2"], 9)):
        for l in range(2):
            for v in range(nv):
                for k in range(8):
                    out[n] = w[l][k * 128:(k + 1) * 128, v * 1024:(v + 1) * 1024]
                    n += 1
    return out


def pack_vec(a):
    cols, n = columns()
    out = np.zeros((P, n), np.float32)

    def put(name, v):
        s, w = cols[name]
        out[:, s:s + w] = np.ascontiguousarray(v).reshape(w, P).T

    put("c", a["c"])
    put("c2", a["c_2"])
    put("ada_b", a["ada_b"])
    put("mix_g", a["norm_mix_g"])
    put("ffn_g", a["norm_ffn_g"])
    put("cw", a["ev_conv_w"])
    put("cb", a["ev_conv_b"])
    put("ba", a["ev_ba"])
    put("bx", a["ev_bx"])
    put("lam", a["ev_lam"])
    for n_, k in (("evq", "ev_qn_g"), ("evk", "ev_kn_g"), ("odq", "od_qn_g"), ("odk", "od_kn_g")):
        put(n_, np.concatenate([a[k][0], a[k][0]]))
    put("fcw", a["ffn_conv_w"])
    put("fcb", a["ffn_conv_b"])
    put("pre", a["norm_pre_2"])
    put("post", a["norm_post_2"])
    put("b_mod", a["b_mod_2"])
    put("mq", a["mla_q_norm_2"])
    put("mkv", a["mla_kv_norm_2"])
    s, w = cols["sinks"]
    out[:, s:s + w] = a["od_sinks"][0][None, :]
    return out


def kernel(**inputs):
    import concourse.bacc as bacc
    from concourse.bass_utils import run_bass_kernel_spmd as run

    a = {k: np.asarray(v) for k, v in inputs.items()}
    consts = const_arrays()
    wax = np.zeros((P, 8, P), np.float32)
    for g, k in enumerate(("ev_wa", "ev_wx")):
        for n in range(8):
            o = 64 * (n % 2)
            wax[o:o + 64, 4 * g + n // 2, o:o + 64] = a[k][0, n]
    arrays = {
        "xt": np.ascontiguousarray(a["x"][0].T.reshape(8, P, S).transpose(1, 0, 2)),
        "wst": pack_stream(a),
        "mst": pack_mod(a),
        "vec": pack_vec(a),
        "cst": np.concatenate([consts[n] for n, _ in CONST_WIDTHS], axis=1),
        "trig": consts["trig"],
        "oh": onehots(),
        "flip": np.ascontiguousarray(np.eye(P, dtype=np.float32)[::-1]),
        "tab": np.ascontiguousarray(a["rel_bias_2"]),
        "wax": wax,
    }
    nc = bacc.Bacc("TRN2", target_bir_lowering=False, num_devices=1)
    aps = {n: nc.dram_tensor(n, v.shape, F32, kind="ExternalInput").ap() for n, v in arrays.items()}
    o = nc.dram_tensor("out", (P, 8, S), F32, kind="ExternalOutput").ap()
    sc = nc.dram_tensor("scratch", (P, 16, 416), F32, kind="Internal").ap()
    bv = nc.dram_tensor("bvec", (16, 704), F32, kind="Internal").ap()
    program(nc, out=o, bvec=bv, scratch=sc, **aps)
    r = run(nc, [arrays], core_ids=[0])
    got = np.asarray(r.results[0]["out"])
    return np.ascontiguousarray(got.transpose(1, 0, 2).reshape(1024, S).T)[None]
```
